# Optimizing a Trainium2 kernel written in Bass

```python
import math
import jax, jax.numpy as jnp
from jax import lax
import numpy as np

D_MODEL = 1024
BATCH = 1
SEQ = 1024
DEPTH = 1

GM_WIDTH = D_MODEL // 2
GM_GROUPS = 8
GM_GROUP_DIM = GM_WIDTH // GM_GROUPS
GM_CHUNK = 128

NSA_HEADS = 8
NSA_KV_GROUPS = 2
NSA_REP = NSA_HEADS // NSA_KV_GROUPS
HEAD_DIM = (D_MODEL - GM_WIDTH) // NSA_HEADS
Q_DIM = NSA_HEADS * HEAD_DIM
KV_DIM = NSA_KV_GROUPS * HEAD_DIM
MIX_WIDTH = GM_WIDTH + Q_DIM
CMP_BLOCK = 32
CMP_STRIDE = 16
CMP_HIDDEN = 256
SLC_BLOCK = 64
SLC_TOPN = 16
WINDOW = 512
Q_BLOCK = 128
FORCE_SCORE = 1e9
ATTN_SCALE = HEAD_DIM ** -0.5
IN_SIZES = (GM_WIDTH, GM_WIDTH, Q_DIM, KV_DIM, KV_DIM, KV_DIM, KV_DIM, KV_DIM, KV_DIM, 3 * NSA_HEADS)
IN_COLS = sum(IN_SIZES)

N_EXPERTS = 32
TOP_K = 4
D_FF = D_MODEL
SWIGLU_LIMIT = 7.0
SWIGLU_ALPHA = 1.702
MOE_BLOCK = 128

N_MOD = 6
EPS = 1e-6

kernel_name = "hybrid_gmlp_nsa_moe_adaln"

def rmsnorm(x, g):
    x32 = x.astype(jnp.float32)
    y = x32 * lax.rsqrt(jnp.mean(x32 * x32, axis=-1, keepdims=True) + EPS)
    return (y * g.astype(jnp.float32)).astype(x.dtype)

def masked_softmax(s, mask):
    s = jnp.where(mask, s, -jnp.inf)
    m = jnp.max(s, axis=-1, keepdims=True)
    m = jnp.where(jnp.isfinite(m), m, 0.0)
    p = jnp.where(mask, jnp.exp(s - m), 0.0)
    return p / jnp.maximum(jnp.sum(p, axis=-1, keepdims=True), 1e-30)

def alibi_slopes():
    h = jnp.arange(NSA_HEADS, dtype=jnp.float32)
    return jnp.exp2(-8.0 * (h + 1.0) / NSA_HEADS).reshape(NSA_KV_GROUPS, NSA_REP)

def gmlp_mixer(u, v, w_s, b_s, g_sgu):
    B_, S_, _ = v.shape
    u = jax.nn.gelu(u)
    v = jax.nn.gelu(v).reshape(B_, S_, GM_GROUPS, GM_GROUP_DIM)
    v = rmsnorm(v, g_sgu.reshape(GM_GROUPS, GM_GROUP_DIM))
    vc = v.reshape(B_, S_ // GM_CHUNK, GM_CHUNK, GM_GROUPS, GM_GROUP_DIM)
    causal = jnp.tril(jnp.ones((GM_CHUNK, GM_CHUNK), dtype=bool))
    ws = jnp.where(causal[None], w_s, 0.0)
    z = jnp.einsum('gij,bcjgd->bcigd', ws, vc) + b_s.T[:, :, None]
    return u * z.reshape(B_, S_, GM_WIDTH)

def compress(k, pe, w1, w2):
    B_, S_, G_, D_ = k.shape
    ratio = CMP_BLOCK // CMP_STRIDE
    n_chunk = S_ // CMP_STRIDE
    n_cmp = n_chunk - ratio + 1
    c = k.reshape(B_, n_chunk, CMP_STRIDE, G_, D_)
    blocks = jnp.concatenate([c[:, j:j + n_cmp] for j in range(ratio)], axis=2)
    blocks = blocks + pe[:, None, :]
    flat = blocks.transpose(0, 3, 1, 2, 4).reshape(B_, G_, n_cmp, CMP_BLOCK * D_)
    return jax.nn.gelu(flat @ w1) @ w2

def nsa_mixer(q, k_c, v_c, k_s, v_s, k_w, v_w, gates, pe_k, w1_k, w2_k, pe_v, w1_v, w2_v):
    B_, S_ = q.shape[0], q.shape[1]
    G, R, HD = NSA_KV_GROUPS, NSA_REP, HEAD_DIM
    slopes = alibi_slopes()
    qh = q.reshape(B_, S_, G, R, HD).transpose(0, 2, 3, 1, 4)
    gh = gates.reshape(B_, S_, G, R, 3).transpose(0, 2, 3, 1, 4)

    kc = compress(k_c, pe_k, w1_k, w2_k)
    vc = compress(v_c, pe_v, w1_v, w2_v)
    n_cmp = kc.shape[2]
    cend = jnp.arange(n_cmp) * CMP_STRIDE + CMP_BLOCK - 1

    n_blk = S_ // SLC_BLOCK
    n_sel = min(SLC_TOPN, n_blk)
    ksb = k_s.transpose(0, 2, 1, 3).reshape(B_, G, n_blk, SLC_BLOCK, HD)
    vsb = v_s.transpose(0, 2, 1, 3).reshape(B_, G, n_blk, SLC_BLOCK, HD)
    blk = jnp.arange(n_blk)
    cst = jnp.arange(n_cmp) * CMP_STRIDE
    overlap = ((cst[:, None] < blk[None] * SLC_BLOCK + SLC_BLOCK) &
               (blk[None] * SLC_BLOCK < cst[:, None] + CMP_BLOCK)).astype(jnp.float32)

    kw_pad = jnp.pad(k_w.transpose(0, 2, 1, 3), ((0, 0), (0, 0), (WINDOW, 0), (0, 0)))
    vw_pad = jnp.pad(v_w.transpose(0, 2, 1, 3), ((0, 0), (0, 0), (WINDOW, 0), (0, 0)))
    bi = jnp.arange(B_)[:, None, None, None]
    gi = jnp.arange(G)[None, :, None, None]

    def query_block(qb):
        q0 = qb * Q_BLOCK
        t = q0 + jnp.arange(Q_BLOCK)
        qblk = lax.dynamic_slice_in_dim(qh, q0, Q_BLOCK, axis=3)
        gblk = lax.dynamic_slice_in_dim(gh, q0, Q_BLOCK, axis=3)

        dist_c = (t[:, None] - cend[None]).astype(jnp.float32)
        s_c = jnp.einsum('bgrqd,bgcd->bgrqc', qblk, kc, preferred_element_type=jnp.float32) * ATTN_SCALE
        s_c = s_c - slopes[None, :, :, None, None] * dist_c
        p_c = masked_softmax(s_c, dist_c >= 0)
        o_c = jnp.einsum('bgrqc,bgcd->bgrqd', p_c.astype(vc.dtype), vc)

        imp = jnp.einsum('bgrqc,cj->bgqj', p_c, overlap)
        cur = t // SLC_BLOCK
        forced = (blk[None] == 0) | (blk[None] == cur[:, None]) | (blk[None] == cur[:, None] - 1)
        imp = jnp.where(forced, FORCE_SCORE, imp)
        imp = jnp.where(blk[None] * SLC_BLOCK <= t[:, None], imp, -jnp.inf)
        top_val, idx = lax.top_k(imp, n_sel)
        sel_ok = jnp.isfinite(top_val)
        ks = ksb[bi, gi, idx]
        vs = vsb[bi, gi, idx]
        pos = idx[..., None] * SLC_BLOCK + jnp.arange(SLC_BLOCK)
        dist_s = t[None, None, :, None, None] - pos
        mask_s = (dist_s >= 0) & sel_ok[..., None]
        s_s = jnp.einsum('bgrqd,bgqnld->bgrqnl', qblk, ks, preferred_element_type=jnp.float32) * ATTN_SCALE
        s_s = s_s - slopes[None, :, :, None, None, None] * dist_s[:, :, None].astype(jnp.float32)
        s_s = s_s.reshape(B_, G, R, Q_BLOCK, n_sel * SLC_BLOCK)
        mask_s = mask_s[:, :, None].reshape(B_, G, 1, Q_BLOCK, n_sel * SLC_BLOCK)
        p_s = masked_softmax(s_s, mask_s)
        o_s = jnp.einsum('bgrqm,bgqmd->bgrqd', p_s.astype(vs.dtype),
                         vs.reshape(B_, G, Q_BLOCK, n_sel * SLC_BLOCK, HD))

        kw = lax.dynamic_slice_in_dim(kw_pad, q0, Q_BLOCK + WINDOW, axis=2)
        vw = lax.dynamic_slice_in_dim(vw_pad, q0, Q_BLOCK + WINDOW, axis=2)
        spos = q0 - WINDOW + jnp.arange(Q_BLOCK + WINDOW)
        dist_w = t[:, None] - spos[None]
        mask_w = (spos[None] >= 0) & (dist_w >= 0) & (dist_w < WINDOW)
        s_w = jnp.einsum('bgrqd,bgkd->bgrqk', qblk, kw, preferred_element_type=jnp.float32) * ATTN_SCALE
        s_w = s_w - slopes[None, :, :, None, None] * dist_w.astype(jnp.float32)
        p_w = masked_softmax(s_w, mask_w)
        o_w = jnp.einsum('bgrqk,bgkd->bgrqd', p_w.astype(vw.dtype), vw)

        return gblk[..., 0:1] * o_c + gblk[..., 1:2] * o_s + gblk[..., 2:3] * o_w

    out = lax.map(query_block, jnp.arange(S_ // Q_BLOCK))
    return out.transpose(1, 0, 4, 2, 3, 5).reshape(B_, S_, Q_DIM)

def moe(h, w_router, b_router, w_gu, b_gu, w_dn, b_dn):
    B_, S_, D_ = h.shape
    T = B_ * S_
    TK = T * TOP_K
    hf = h.reshape(T, D_)
    logits = (hf @ w_router + b_router).astype(jnp.float32)
    top_logits, top_idx = lax.top_k(logits, TOP_K)
    wts = jax.nn.softmax(top_logits, axis=-1)
    e_flat = top_idx.reshape(-1)
    tok_flat = jnp.repeat(jnp.arange(T), TOP_K)
    order = jnp.argsort(e_flat)
    e_sorted = e_flat[order]
    tok_sorted = tok_flat[order]
    w_sorted = wts.reshape(-1)[order]
    counts = jnp.bincount(e_flat, length=N_EXPERTS)
    padded = (counts + MOE_BLOCK - 1) // MOE_BLOCK * MOE_BLOCK
    start = jnp.cumsum(counts) - counts
    pstart = jnp.cumsum(padded) - padded
    pend = pstart + padded
    dest = pstart[e_sorted] + (jnp.arange(TK) - start[e_sorted])
    P = (TK + MOE_BLOCK - 1) // MOE_BLOCK * MOE_BLOCK + N_EXPERTS * MOE_BLOCK
    n_rb = P // MOE_BLOCK
    xd = jnp.zeros((P, D_), h.dtype).at[dest].set(hf[tok_sorted])
    block_e = jnp.minimum(jnp.searchsorted(pend, jnp.arange(n_rb) * MOE_BLOCK, side='right'), N_EXPERTS - 1)

    def expert_block(args):
        xb, e = args
        gu = xb @ w_gu[e] + b_gu[e]
        x_glu = jnp.minimum(gu[:, 0::2], SWIGLU_LIMIT)
        x_lin = jnp.clip(gu[:, 1::2], -SWIGLU_LIMIT, SWIGLU_LIMIT)
        act = x_glu * jax.nn.sigmoid(SWIGLU_ALPHA * x_glu) * (x_lin + 1.0)
        return act @ w_dn[e] + b_dn[e]

    yd = lax.map(expert_block, (xd.reshape(n_rb, MOE_BLOCK, D_), block_e)).reshape(P, D_)
    y = yd[dest] * w_sorted[:, None].astype(h.dtype)
    out = jnp.zeros((T, D_), h.dtype).at[tok_sorted].add(y)
    return out.reshape(B_, S_, D_)

def setup_inputs(seed: int = 0) -> dict:
    key = jax.random.key(seed)
    ks = jax.random.split(key, 26)
    f32 = jnp.float32
    L, D = DEPTH, D_MODEL
    nrm = lambda k, shape, scale: jax.random.normal(k, shape, f32) * scale
    return {
        "x": nrm(ks[0], (BATCH, SEQ, D), 1.0),
        "c": nrm(ks[1], (BATCH, D), 1.0),
        "w_ada": nrm(ks[2], (L, D, N_MOD * D), 0.5 * D ** -0.5),
        "b_ada": nrm(ks[3], (L, N_MOD * D), 0.02),
        "g_mix_norm": 1.0 + nrm(ks[4], (L, D), 0.05),
        "w_in": nrm(ks[5], (L, D, IN_COLS), D ** -0.5),
        "gm_w_s": nrm(ks[6], (L, GM_GROUPS, GM_CHUNK, GM_CHUNK), GM_CHUNK ** -0.5),
        "gm_b_s": 1.0 + nrm(ks[7], (L, GM_GROUPS, GM_CHUNK), 0.1),
        "gm_norm_g": 1.0 + nrm(ks[8], (L, GM_WIDTH), 0.05),
        "cmp_pe_k": nrm(ks[9], (L, CMP_BLOCK, HEAD_DIM), 0.1),
        "cmp_w1_k": nrm(ks[10], (L, CMP_BLOCK * HEAD_DIM, CMP_HIDDEN), (CMP_BLOCK * HEAD_DIM) ** -0.5),
        "cmp_w2_k": nrm(ks[11], (L, CMP_HIDDEN, HEAD_DIM), CMP_HIDDEN ** -0.5),
        "cmp_pe_v": nrm(ks[12], (L, CMP_BLOCK, HEAD_DIM), 0.1),
        "cmp_w1_v": nrm(ks[13], (L, CMP_BLOCK * HEAD_DIM, CMP_HIDDEN), (CMP_BLOCK * HEAD_DIM) ** -0.5),
        "cmp_w2_v": nrm(ks[14], (L, CMP_HIDDEN, HEAD_DIM), CMP_HIDDEN ** -0.5),
        "w_out": nrm(ks[15], (L, MIX_WIDTH, D), MIX_WIDTH ** -0.5),
        "g_ffn_norm": 1.0 + nrm(ks[16], (L, D), 0.05),
        "w_router": nrm(ks[17], (L, D, N_EXPERTS), D ** -0.5),
        "b_router": nrm(ks[18], (L, N_EXPERTS), 0.01),
        "w_gate_up": nrm(ks[19], (L, N_EXPERTS, D, 2 * D_FF), D ** -0.5),
        "b_gate_up": nrm(ks[20], (L, N_EXPERTS, 2 * D_FF), 0.01),
        "w_down": nrm(ks[21], (L, N_EXPERTS, D_FF, D), D_FF ** -0.5),
        "b_down": nrm(ks[22], (L, N_EXPERTS, D), 0.01),
        "g_final": 1.0 + nrm(ks[23], (D,), 0.05),
    }

def reference(x, c, w_ada, b_ada, g_mix_norm, w_in, gm_w_s, gm_b_s, gm_norm_g,
              cmp_pe_k, cmp_w1_k, cmp_w2_k, cmp_pe_v, cmp_w1_v, cmp_w2_v, w_out,
              g_ffn_norm, w_router, b_router, w_gate_up, b_gate_up, w_down, b_down, g_final):
    B_, S_, D_ = x.shape
    split_at = [int(v) for v in np.cumsum(IN_SIZES)[:-1]]
    for l in range(DEPTH):
        mod = (c @ w_ada[l] + b_ada[l]).reshape(B_, N_MOD, D_)
        sh1, sc1, gt1, sh2, sc2, gt2 = [mod[:, i, None, :] for i in range(N_MOD)]

        h = rmsnorm(x, g_mix_norm[l]) * (1.0 + sc1) + sh1
        z = h @ w_in[l]
        u, v, q, kc, vc, ksl, vsl, kw, vw, gl = jnp.split(z, split_at, axis=-1)
        y_gm = gmlp_mixer(u, v, gm_w_s[l], gm_b_s[l], gm_norm_g[l])
        r4 = lambda a: a.reshape(B_, S_, NSA_KV_GROUPS, HEAD_DIM)
        gates = jax.nn.sigmoid(gl).reshape(B_, S_, NSA_HEADS, 3)
        y_nsa = nsa_mixer(q.reshape(B_, S_, NSA_HEADS, HEAD_DIM), r4(kc), r4(vc), r4(ksl), r4(vsl),
                          r4(kw), r4(vw), gates, cmp_pe_k[l], cmp_w1_k[l], cmp_w2_k[l],
                          cmp_pe_v[l], cmp_w1_v[l], cmp_w2_v[l])
        mix = jnp.concatenate([y_gm, y_nsa], axis=-1) @ w_out[l]
        x = x + gt1 * mix

        h2 = rmsnorm(x, g_ffn_norm[l]) * (1.0 + sc2) + sh2
        x = x + gt2 * moe(h2, w_router[l], b_router[l], w_gate_up[l], b_gate_up[l], w_down[l], b_down[l])
    return rmsnorm(x, g_final)


_drawn_inputs = setup_inputs


def setup_inputs(seed=0):
    import zlib

    import numpy as np

    out = dict(_drawn_inputs(seed))
    spreads = {}
    factors = {'gm_norm_g': 2.72,
     'cmp_pe_k': 16.516,
     'b_router': 2.933,
     'b_gate_up': 8.0,
     'b_down': 24.818,
     'cmp_pe_v': 2.861}
    for name, (base, spread) in spreads.items():
        noise = np.random.default_rng([zlib.crc32(name.encode()), seed]).standard_normal(out[name].shape)
        drawn = base * np.exp(spread * noise) if base else spread * noise
        out[name] = __import__('jax').numpy.asarray(drawn.astype(out[name].dtype))
    for name, factor in factors.items():
        out[name] = (out[name] * factor).astype(out[name].dtype)
    return out
```

```python
import numpy as np
import concourse.bass as bass
from concourse import mybir
from contextlib import ExitStack

P = 128
D = 1024
SEQ = 1024
KD = D // P
TILES = SEQ // P
N_MOD = 6
GM_WIDTH = 512
GM_GROUPS = 8
GM_DIM = GM_WIDTH // GM_GROUPS
HEADS = 8
KV_GROUPS = 2
REP = HEADS // KV_GROUPS
HD = 64
CMP_BLOCK = 32
CMP_STRIDE = 16
CMP_HIDDEN = 256
N_CMP = SEQ // CMP_STRIDE - 1
NCP = N_CMP + 1
WIN_TILES = 512 // P
ATTN_SCALE = HD ** -0.5
E = 32
TOPK = 4
CAP = 384
SUBS = CAP // P
SLOTS = CAP * -(-SEQ // CAP)
LIST_ROWS = E * SLOTS + CAP
STEP = 32
WIDTHS = list(range(P, CAP + 1, STEP))
PASS_COLS = 8
T_EXPERT, T_START, T_WIDTH, T_SUBS, T_PASSES = range(5)
MAX_PASSES = E + (TOPK * SEQ) // CAP
LIMIT = 7.0
ALPHA = 1.702
EPS = 1e-6
NEG = -1e30

C_U, C_V, C_Q, C_KC, C_VC, C_KS, C_VS, C_KW, C_VW, C_GL = 0, 512, 1024, 1536, 1664, 1792, 1920, 2048, 2176, 2304
IN_COLS = 2328
MISC = 2 * P + 3 * HEADS

f32 = mybir.dt.float32
bf16 = mybir.dt.bfloat16
i32 = mybir.dt.int32
u32 = mybir.dt.uint32
ALU = mybir.AluOpType
ACT = mybir.ActivationFunctionType
AX = mybir.AxisListType


def bc_mid(ap, n):
    return ap.unsqueeze(1).to_broadcast([ap.shape[0], n, ap.shape[1]])


def bc_last(ap, n):
    return ap.unsqueeze(2).to_broadcast([ap.shape[0], ap.shape[1], n])


class Chain:

    def __init__(self, eng, sem):
        self.eng, self.sem, self.base, self.n = eng, sem, 0, 0

    def at(self, base):
        self.base, self.n = base, 0

    def link(self, ins):
        ins.then_inc(self.sem, 1)
        self.n += 1
        self.eng.wait_ge(self.sem, self.base + self.n)


def layer_kernel(nc, x, c, w_ada, b_ada, g_mix_norm, w_in, gm_w_s, gm_b_s, gm_norm_g, cmp_pe_k, cmp_w1_k, cmp_w2_k,
                 cmp_pe_v, cmp_w1_v, cmp_w2_v, w_out, g_ffn_norm, w_router, b_router, w_gate_up, b_gate_up, w_down,
                 b_down, g_final, k_ident, k_masks, k_cmask, k_kside, k_qside, k_upper, k_expert, k_pairs, out):
    ctx = ExitStack()
    with ctx:
        sem = lambda name: ctx.enter_context(nc.semaphore(name))
        psum = ctx.enter_context(nc.psum_tensor("psum", [P, 8 * 512], f32))
        pb = [psum[:, i * 512:(i + 1) * 512] for i in range(8)]
        x1_d = nc.dram_tensor("x1_rows", [SEQ, D], f32, kind="Internal").ap()
        xn_d = nc.dram_tensor("xn_rows", [SEQ, D], f32, kind="Internal").ap()
        y_d = nc.dram_tensor("expert_rows", [SEQ * TOPK, D], f32, kind="Internal").ap()
        mod_d = nc.dram_tensor("mod_vector", [N_MOD * D], f32, kind="Internal").ap()
        list_d = nc.dram_tensor("slot_list", [LIST_ROWS, 2], i32, kind="Internal").ap()
        pass_d = nc.dram_tensor("pass_table", [P, PASS_COLS], i32, kind="Internal").ap()

        keep = lambda name, shape, dt=f32: ctx.enter_context(nc.sbuf_tensor(name, shape, dt))
        ident = keep("ident", [P, P])
        vec_t = keep("vec_t", [P, 72])
        mod_t = keep("mod_t", [P, N_MOD * KD])
        scale1 = keep("scale1", [P, KD])
        scale2 = keep("scale2", [P, KD])
        wts = keep("wts", [P, TILES, TOPK])

        stage3 = ExitStack()
        y_rows = stage3.enter_context(nc.sbuf_tensor("y_rows", [P, TILES, D], f32))
        stage2 = ExitStack()
        qT_all = stage2.enter_context(nc.sbuf_tensor("qT_all", [P, REP, SEQ], f32))
        kT_all = stage2.enter_context(nc.sbuf_tensor("kT_all", [P, 4, SEQ], f32))
        misc = stage2.enter_context(nc.sbuf_tensor("misc", [P, TILES, MISC], f32))

        with ExitStack() as s1:
            project_tokens(nc, s1, sem, pb, x, c, w_ada, b_ada, g_mix_norm, g_ffn_norm, w_in, gm_w_s, gm_b_s, gm_norm_g,
                           k_ident, mod_d, ident, vec_t, mod_t, scale1, scale2, y_rows, qT_all, kT_all, misc)
        with ExitStack() as s2:
            attend(nc, s2, sem, psum, cmp_pe_k, cmp_w1_k, cmp_w2_k, cmp_pe_v, cmp_w1_v, cmp_w2_v, k_masks, k_cmask,
                   k_kside, k_qside, ident, y_rows, qT_all, kT_all, misc)
        stage2.close()
        with ExitStack() as s3:
            route(nc, s3, sem, psum, x, w_out, w_router, b_router, k_upper, k_expert, k_pairs, mod_d, list_d, pass_d,
                  x1_d, xn_d, ident, mod_t, scale2, y_rows, wts)
        stage3.close()
        with ExitStack() as s4:
            experts(nc, s4, sem, psum, w_gate_up, b_gate_up, w_down, b_down, list_d, pass_d, xn_d, y_d,
                    ident, mod_t, scale2)
        with ExitStack() as s5:
            combine(nc, s5, sem, g_final, mod_d, x1_d, y_d, wts, out)


ADA_COLS = 256
ADA_FIRST = 2 * D // ADA_COLS


def project_tokens(nc, ctx, sem, pb, x, c, w_ada, b_ada, g_mix_norm, g_ffn_norm, w_in, gm_w_s, gm_b_s, gm_norm_g,
                   k_ident, mod_d, ident, vec_t, mod_t, scale1, scale2, y_rows, qT_all, kT_all, misc):
    sb = lambda name, shape, dt=f32: ctx.enter_context(nc.sbuf_tensor(name, shape, dt))
    w_sb = sb("w_in_sb", [P, KD, IN_COLS])
    ada = [sb(f"ada{i}", [P, KD, ADA_COLS]) for i in range(2)]
    xt = [sb(f"xt{i}", [P, D]) for i in range(2)]
    hT = [sb(f"hT{i}", [P, KD, P]) for i in range(2)]
    vecs = sb("vecs", [72, P])
    ws = y_rows[:, TILES - 1, :].rearrange("p (g j) -> p g j", g=GM_GROUPS)
    wsT = sb("wsT", [P, GM_GROUPS, P])
    bs_rows = sb("bs_rows", [GM_GROUPS, P])
    bsT = sb("bsT", [P, GM_GROUPS])
    gm_g = sb("gm_g", [P, GM_WIDTH])
    sq = sb("sq", [P, D], bf16)
    ms = sb("ms", [P, 2])
    rstd = sb("rstd", [P, 2])
    v_act = sb("v_act", [P, GM_WIDTH])
    u_act = sb("u_act", [P, GM_WIDTH])
    vn = sb("vn", [P, GM_WIDTH])
    zb = sb("zb", [P, GM_WIDTH])
    vms = sb("vms", [P, GM_GROUPS])
    vrs = sb("vrs", [P, GM_GROUPS])
    nhalf = sb("nhalf", [P, GM_GROUPS])
    eps = sb("eps", [P, 1 + GM_GROUPS])
    psX = pb[0:2]
    psV, psU, psM, psQ, psK, psZ = pb[2:8]
    MOD0 = 288

    s_vec, s_gm, s_win = sem("vec_loaded"), sem("gm_loaded"), sem("w_in_loaded")
    s_x = [sem(f"x_loaded{i}") for i in range(2)]
    s_ada = [sem(f"ada_loaded{i}") for i in range(2)]
    s_vecT, s_vecT_sb, s_wsT, s_wsT_sb = sem("vecT_ps"), sem("vecT_sb"), sem("wsT_ps"), sem("wsT_sb")
    s_wsc = sem("ws_causal")
    s_adafree, s_mod = sem("ada_used"), sem("mod_sb")
    s_ms, s_xs, s_xTps, s_hT = sem("ms_ready"), sem("xs_ready"), sem("xT_ps"), sem("hT_ready")
    s_v, s_u, s_m, s_q, s_k, s_z = (sem(n) for n in ("v_ps", "u_ps", "misc_ps", "q_ps", "k_ps", "z_ps"))
    s_vact, s_uact, s_vn, s_zused = sem("v_act"), sem("u_act"), sem("vn_ready"), sem("z_used")
    s_mused, s_qused, s_kused = sem("misc_used"), sem("q_used"), sem("k_used")
    s_chain, s_modst = sem("dve_chain1"), sem("mod_stored")
    s_rstd, s_vms, s_vrs = sem("rstd_ready"), sem("v_sums"), sem("v_rstd")
    s_vmean, s_mseps, s_nhalf = sem("v_means"), sem("ms_eps"), sem("nhalf_set")
    s_modT, s_modrow = sem("modT_ps"), sem("mod_rows_ready")

    x_t = x.rearrange("(t p) d -> t p d", p=P)
    w_ada_v = w_ada.rearrange("(k p) n -> p k n", p=P)
    w_in_v = w_in.rearrange("(k p) n -> p k n", p=P)

    def tiles(eng, body):
        with eng.Fori(0, TILES // 2 - 1) as i:
            body(2 * i, 0, i, True, True)
            body(2 * i + 1, 1, i, True, True)
        body(TILES - 2, 0, TILES // 2 - 1, True, False)
        body(TILES - 1, 1, TILES // 2 - 1, False, False)

    block = ctx.enter_context(nc.Block())

    @block.sync
    def _(sp):
        sp.dma_start(ident[:], k_ident).then_inc(s_vec, 16)
        sp.dma_start(vecs[0:48, :], b_ada.rearrange("(r p) -> r p", p=P)).then_inc(s_vec, 16)
        sp.dma_start(vecs[48:56, :], g_mix_norm.rearrange("(r p) -> r p", p=P)).then_inc(s_vec, 16)
        sp.dma_start(vecs[56:64, :], g_ffn_norm.rearrange("(r p) -> r p", p=P)).then_inc(s_vec, 16)
        sp.dma_start(vecs[64:72, :], c.rearrange("(r p) -> r p", p=P)).then_inc(s_vec, 16)
        for i in range(2):
            sp.dma_start(ada[i][:], w_ada_v[:, :, i * ADA_COLS:(i + 1) * ADA_COLS]).then_inc(s_ada[i], 16)
            sp.dma_start(xt[i][:], x_t[i]).then_inc(s_x[i], 16)
        for n in range(2, ADA_FIRST):
            sp.wait_ge(s_adafree, n - 1)
            sp.dma_start(ada[n % 2][:], w_ada_v[:, :, n * ADA_COLS:(n + 1) * ADA_COLS]).then_inc(s_ada[n % 2], 16)
        for k in range(KD):
            sp.dma_start(w_sb[:, k, 0:C_Q], w_in_v[:, k, 0:C_Q]).then_inc(s_win, 16)
            sp.dma_start(w_sb[:, k, C_KC:IN_COLS], w_in_v[:, k, C_KC:IN_COLS]).then_inc(s_win, 16)
            for g in range(KV_GROUPS):
                sp.dma_start(w_sb[:, k, C_Q:C_KC].rearrange("p (j g d) -> p g j d", g=KV_GROUPS, j=REP)[:, g, :, :],
                             w_in_v[:, k, C_Q:C_KC].rearrange("p (g j d) -> p g j d", g=KV_GROUPS, j=REP)[:, g, :, :]
                             ).then_inc(s_win, 16)
        for n in range(2):
            sp.wait_ge(s_adafree, ADA_FIRST - 1 + n)
            m = ADA_FIRST + n
            sp.dma_start(ada[n][:], w_ada_v[:, :, m * ADA_COLS:(m + 1) * ADA_COLS]).then_inc(s_ada[n], 16)

        def body(t, par, i, nxt, nxt2):
            if nxt2:
                sp.wait_ge(s_xTps, t + 1)
                sp.dma_start(xt[par][:], x_t[bass.ds(t + 2, 1)].rearrange("a p d -> (a p) d")).then_inc(s_x[par], 16)
            if nxt:
                for n in range(2):
                    sp.wait_ge(s_adafree, ADA_FIRST + 2 * t + n + 1)
                    sp.dma_start(ada[n][:], w_ada_v[:, :, bass.ds((2 * t + 2 + n + ADA_FIRST) * ADA_COLS, ADA_COLS)]
                                 ).then_inc(s_ada[n], 16)
        tiles(sp, body)
        sp.wait_ge(s_modrow, 1)
        sp.dma_start(mod_d.rearrange("(r p) -> r p", p=P), vecs[0:48, :]).then_inc(s_modst, 16)
        sp.wait_ge(s_modst, 16)

    @block.gpsimd
    def _(pool):
        pool.dma_start(ws, gm_w_s.rearrange("g i j -> i g j")).then_inc(s_gm, 16)
        pool.dma_start(bs_rows[:], gm_b_s).then_inc(s_gm, 16)
        pool.dma_start(gm_g[:], gm_norm_g.rearrange("(a n) -> a n", a=1).partition_broadcast(P)).then_inc(s_gm, 16)
        pool.wait_ge(s_gm, 48)
        nc.gpsimd.affine_select(out=ws, in_=ws, compare_op=ALU.is_ge, fill=0.0, base=0,
                                pattern=[[0, GM_GROUPS], [-1, P]], channel_multiplier=1).then_inc(s_wsc, 1)

        def x_rstd(t, par):
            pool.wait_ge(s_ms, t + 1)
            nc.gpsimd.tensor_tensor(ms[:, par:par + 1], ms[:, par:par + 1], eps[:, 0:1], ALU.add).then_inc(s_mseps, 1)
            pool.wait_ge(s_mseps, t + 1)
            nc.gpsimd.tensor_tensor(rstd[:, par:par + 1], ms[:, par:par + 1], nhalf[:, 0:1],
                                    ALU.pow).then_inc(s_rstd, 1)
        nc.gpsimd.memset(nhalf[:], -0.5).then_inc(s_nhalf, 1)
        nc.gpsimd.memset(eps[:, 0:1], EPS).then_inc(s_nhalf, 1)
        nc.gpsimd.memset(eps[:, 1:1 + GM_GROUPS], EPS * GM_DIM).then_inc(s_nhalf, 1)
        pool.wait_ge(s_nhalf, 3)
        x_rstd(0, 0)
        x_rstd(1, 1)

        def body(t, par, i, nxt, nxt2):
            pool.wait_ge(s_vms, t + 1)
            nc.gpsimd.tensor_tensor(vms[:], vms[:], eps[:, 1:1 + GM_GROUPS], ALU.add).then_inc(s_vmean, 1)
            pool.wait_ge(s_vmean, t + 1)
            nc.gpsimd.tensor_tensor(vrs[:], vms[:], nhalf[:], ALU.pow).then_inc(s_vrs, 1)
            if nxt2:
                x_rstd(t + 2, par)
        tiles(pool, body)

    @block.tensor
    def _(pe):
        pe.wait_ge(s_vec, 80)
        nc.tensor.transpose(psX[0][:, 0:72], vecs[:, :], ident[0:72, 0:72]).then_inc(s_vecT, 1)
        pe.wait_ge(s_vecT_sb, 1)

        def modulate(par, col, count):
            pe.wait_ge(s_ada[par], count)
            for m in range(ADA_COLS // P):
                for k in range(KD):
                    last = nc.tensor.matmul(psM[:, col + m:col + m + 1], ada[par][:, k, m * P:(m + 1) * P],
                                            vec_t[:, 64 + k:65 + k], start=(k == 0), stop=(k == KD - 1))
            return last

        for n in range(ADA_FIRST):
            modulate(n % 2, MOD0 + 2 * n, 16 * (n // 2 + 1)).then_inc(s_adafree, 1)
        pe.wait_ge(s_wsc, 1)
        for g in range(GM_GROUPS):
            nc.tensor.transpose(pb[2 + g // 4][:, (g % 4) * P:(g % 4 + 1) * P], ws[:, g, :], ident[:])
        nc.tensor.transpose(psQ[:, 0:GM_GROUPS], bs_rows[:, :], ident[0:GM_GROUPS, 0:GM_GROUPS]).then_inc(s_wsT, 1)

        def transpose_x(t, par):
            pe.wait_ge(s_xs, t + 1)
            pe.wait_ge(s_hT, t)
            for k in range(KD):
                last = nc.tensor.transpose(psX[k // 4][:, (k % 4) * P:(k % 4 + 1) * P], xt[par][:, k * P:(k + 1) * P],
                                           ident[:])
            last.then_inc(s_xTps, 1)

        transpose_x(0, 0)
        pe.wait_ge(s_win, 4 * 16 * KD)
        pe.wait_ge(s_wsT_sb, 1)
        pe.wait_ge(s_mod, 1)

        def body(t, par, i, nxt, nxt2):
            if nxt:
                transpose_x(t + 1, 1 - par)
            pe.wait_ge(s_hT, t + 1)
            for ps, c0, used, done in ((psV, C_V, s_vact, s_v), (psU, C_U, s_uact, s_u)):
                pe.wait_ge(used, t)
                for k in range(KD):
                    last = nc.tensor.matmul(ps[:], hT[par][:, k, :], w_sb[:, k, c0:c0 + 512], start=(k == 0),
                                            stop=(k == KD - 1))
                last.then_inc(done, 1)
            pe.wait_ge(s_mused, t)
            for n in range(2):
                modulate(n, MOD0 + 2 * n, 16 * (ADA_FIRST // 2 + 1 + t)).then_inc(s_adafree, 1)
            for o, c0, n in ((0, C_VS, P), (P, C_VW, P + 3 * HEADS)):
                for k in range(KD):
                    last = nc.tensor.matmul(psM[:, o:o + n], hT[par][:, k, :], w_sb[:, k, c0:c0 + n], start=(k == 0),
                                            stop=(k == KD - 1))
            last.then_inc(s_m, 1)
            pe.wait_ge(s_qused, t)
            for j in range(REP):
                for k in range(KD):
                    last = nc.tensor.matmul(psQ[:, j * P:(j + 1) * P], w_sb[:, k, C_Q + j * P:C_Q + (j + 1) * P],
                                            hT[par][:, k, :], start=(k == 0), stop=(k == KD - 1))
            last.then_inc(s_q, 1)
            pe.wait_ge(s_kused, t)
            for j, c0 in enumerate((C_KC, C_VC, C_KS, C_KW)):
                for k in range(KD):
                    last = nc.tensor.matmul(psK[:, j * P:(j + 1) * P], w_sb[:, k, c0:c0 + P], hT[par][:, k, :],
                                            start=(k == 0), stop=(k == KD - 1))
            last.then_inc(s_k, 1)
            pe.wait_ge(s_vn, t + 1)
            pe.wait_ge(s_zused, t)
            for g in range(GM_GROUPS):
                last = nc.tensor.matmul(psZ[:, g * GM_DIM:(g + 1) * GM_DIM], wsT[:, g, :],
                                        vn[:, g * GM_DIM:(g + 1) * GM_DIM], start=True, stop=True)
            last.then_inc(s_z, 1)
        tiles(pe, body)
        pe.wait_ge(s_mod, 1 + TILES)
        nc.tensor.transpose(psX[0][0:48, 0:P], mod_t[:], ident[:]).then_inc(s_modT, 1)

    @block.scalar
    def _(act):
        def mean_square(t, par, count):
            act.wait_ge(s_x[par], count)
            nc.scalar.activation(sq[:], xt[par][:], ACT.Square, scale=D ** -0.5,
                                 accum_out=ms[:, par:par + 1]).then_inc(s_ms, 1)
            act.wait_ge(s_ms, t + 1)
        mean_square(0, 0, 16)
        mean_square(1, 1, 16)

        def body(t, par, i, nxt, nxt2):
            act.wait_ge(s_v, t + 1)
            act.wait_ge(s_vn, t)
            nc.scalar.activation(v_act[:], psV[:], ACT.Gelu_apprx_tanh).then_inc(s_vact, 1)
            act.wait_ge(s_u, t + 1)
            act.wait_ge(s_zused, t)
            nc.scalar.activation(u_act[:], psU[:], ACT.Gelu_apprx_tanh).then_inc(s_uact, 1)
            if nxt2:
                act.wait_ge(s_xs, t + 1)
                mean_square(t + 2, par, 16 * (i + 2))
        tiles(act, body)

    @block.vector
    def _(dve):
        ch = Chain(dve, s_chain)
        dve.wait_ge(s_vecT, 1)
        nc.vector.tensor_copy(vec_t[:], psX[0][:, 0:72]).then_inc(s_vecT_sb, 1)
        dve.wait_ge(s_vecT_sb, 1)

        def scale_x(t, par):
            dve.wait_ge(s_rstd, t + 1)
            nc.vector.tensor_scalar(xt[par][:], xt[par][:], rstd[:, par:par + 1], None, ALU.mult).then_inc(s_xs, 1)

        def modulate_x(t, par):
            dve.wait_ge(s_xTps, t + 1)
            for k in range(KD):
                last = nc.vector.tensor_scalar(hT[par][:, k, :], psX[k // 4][:, (k % 4) * P:(k % 4 + 1) * P],
                                               scale1[:, k:k + 1], mod_t[:, k:k + 1], ALU.mult, ALU.add)
            last.then_inc(s_hT, 1)

        scale_x(0, 0)
        scale_x(1, 1)
        dve.wait_ge(s_adafree, ADA_FIRST)
        ch.link(nc.vector.tensor_tensor(mod_t[:, 0:16], psM[:, MOD0:MOD0 + 16], vec_t[:, 0:16], ALU.add))
        nc.vector.scalar_tensor_tensor(scale1[:], mod_t[:, KD:2 * KD], 1.0, vec_t[:, 48:56], ALU.add,
                                       ALU.mult).then_inc(s_mod, 1)
        dve.wait_ge(s_mod, 1)
        modulate_x(0, 0)
        dve.wait_ge(s_wsT, 1)
        nc.vector.tensor_copy(wsT[:, 0:4, :], pb[2][:].rearrange("p (g i) -> p g i", g=4))
        nc.vector.tensor_copy(wsT[:, 4:8, :], pb[3][:].rearrange("p (g i) -> p g i", g=4))
        nc.vector.tensor_copy(bsT[:], psQ[:, 0:GM_GROUPS]).then_inc(s_wsT_sb, 1)
        dve.wait_ge(s_gm, 48)
        ch.link(nc.vector.tensor_scalar(gm_g[:], gm_g[:], GM_DIM ** 0.5, None, ALU.mult))
        SETUP = ch.n
        LINKS = 3

        def body(t, par, i, nxt, nxt2):
            ch.at(SETUP + LINKS * t)
            if nxt:
                dve.wait_ge(s_k, t)
                modulate_x(t + 1, 1 - par)
            dve.wait_ge(s_vact, t + 1)
            dve.wait_ge(s_z, t)
            dve.wait_ge(s_zused, t)
            ch.link(nc.vector.tensor_tensor(zb[:], v_act[:], v_act[:], ALU.mult))
            nc.vector.tensor_reduce(vms[:], zb[:].rearrange("p (g d) -> p g d", g=GM_GROUPS), AX.X,
                                    ALU.add).then_inc(s_vms, 1)
            dve.wait_ge(s_vms, t + 1)
            ch.link(nc.vector.tensor_tensor(zb[:], v_act[:], gm_g[:], ALU.mult))
            dve.wait_ge(s_vrs, t + 1)
            nc.vector.tensor_tensor(vn[:].rearrange("p (g d) -> p g d", g=GM_GROUPS),
                                    zb[:].rearrange("p (g d) -> p g d", g=GM_GROUPS), bc_last(vrs[:], GM_DIM),
                                    ALU.mult).then_inc(s_vn, 1)
            dve.wait_ge(s_m, t + 1)
            nc.vector.tensor_tensor(mod_t[:, bass.ds(16 + 4 * t, 4)], psM[:, MOD0:MOD0 + 4],
                                    vec_t[:, bass.ds(16 + 4 * t, 4)], ALU.add).then_inc(s_mod, 1)
            nc.vector.tensor_scalar(misc[:, bass.ds(t, 1), :].rearrange("p a n -> p (a n)"), psM[:, 0:MISC], 1.0, None,
                                    ALU.mult).then_inc(s_mused, 1)
            dve.wait_ge(s_q, t + 1)
            nc.vector.tensor_scalar(qT_all[:, :, bass.ds(t * P, P)], psQ[:].rearrange("p (j n) -> p j n", j=REP),
                                    ATTN_SCALE, None, ALU.mult).then_inc(s_qused, 1)
            dve.wait_ge(s_k, t + 1)
            nc.vector.tensor_scalar(kT_all[:, :, bass.ds(t * P, P)], psK[:].rearrange("p (j n) -> p j n", j=4),
                                    1.0, None, ALU.mult).then_inc(s_kused, 1)
            dve.wait_ge(s_z, t + 1)
            dve.wait_ge(s_uact, t + 1)
            dve.wait_ge(s_vn, t + 1)
            ch.link(nc.vector.tensor_tensor(zb[:].rearrange("p (g d) -> p g d", g=GM_GROUPS),
                                            psZ[:].rearrange("p (g d) -> p g d", g=GM_GROUPS), bc_last(bsT[:], GM_DIM),
                                            ALU.add))
            nc.vector.tensor_tensor(y_rows[:, bass.ds(t, 1), 0:GM_WIDTH].rearrange("p a n -> p (a n)"), zb[:],
                                    u_act[:], ALU.mult).then_inc(s_zused, 1)
            assert ch.n == LINKS
            if nxt2:
                scale_x(t + 2, par)
        tiles(dve, body)
        dve.wait_ge(s_mod, 1 + TILES)
        nc.vector.scalar_tensor_tensor(scale2[:], mod_t[:, 4 * KD:5 * KD], 1.0, vec_t[:, 56:64], ALU.add, ALU.mult)
        dve.wait_ge(s_modT, 1)
        nc.vector.tensor_copy(vecs[0:48, :], psX[0][0:48, 0:P]).then_inc(s_modrow, 1)


WIN0 = SEQ
CMP0 = WIN0 + (WIN_TILES + 1) * P
S_COLS = CMP0 + P
UNITS = TILES * KV_GROUPS
B_CMP, B_SLC, B_WIN = range(3)


def first_window_tile(qt):
    return max(0, qt - WIN_TILES)


def branches(qt):
    return [(B_SLC, 0, (qt + 1) * P), (B_WIN, WIN0, (qt + 1 - first_window_tile(qt)) * P), (B_CMP, CMP0, NCP)]


def tile_groups(qt):
    tiles = [(B_SLC, kt * P, P, kt) for kt in range(qt + 1)]
    first = first_window_tile(qt)
    tiles += [(B_WIN, WIN0 + (kt - first) * P, P, kt) for kt in range(first, qt + 1)]
    tiles += [(B_CMP, CMP0, NCP, 0)]
    return [tiles[n:n + 4] for n in range(0, len(tiles), 4)]


def strips(c0, n):
    while n:
        m = min(n, 512 - c0 % 512)
        yield c0, m
        c0, n = c0 + m, n - m


def attend(nc, ctx, sem, psum, pe_k, w1_k, w2_k, pe_v, w1_v, w2_v, k_masks, k_cmask, k_kside, k_qside, ident, y_rows,
           qT_all, kT_all, misc):
    sb = lambda name, shape, dt=f32: ctx.enter_context(nc.sbuf_tensor(name, shape, dt))
    M2 = CMP_HIDDEN // P
    L2 = CMP_BLOCK // 2
    HALF = P // 2
    KC, VC, KS, KW = range(4)
    w1 = [sb(f"cmp_w1_{i}", [P, L2, CMP_HIDDEN]) for i in range(2)]
    w2 = [sb(f"cmp_w2_{i}", [P, M2, HD]) for i in range(2)]
    pos = [sb(f"cmp_pos_{i}", [L2, P]) for i in range(2)]
    posT = sb("cmp_posT", [P, 2, L2])
    kk = [sb(f"cmp_in_{i}", [P, KV_GROUPS, SEQ]) for i in range(2)]
    hid_b = sb("cmp_bias", [P, 2 * M2])
    hid = sb("cmp_hidden", [P, 2, M2, KV_GROUPS * N_CMP])
    kcT = sb("k_cmpT", [P, NCP])
    vc = sb("v_cmp", [NCP, P])
    masks = sb("masks", [P, 2, P], bf16)
    cmask = sb("cmask", [P, TILES, NCP], bf16)
    kside = sb("kside", [4, SEQ + NCP], bf16)
    qside = sb("qside", [4, KV_GROUPS, SEQ], bf16)
    ident_b = sb("ident_b", [P, P], bf16)
    visible = sb("visible", [P, 3])
    gates = sb("gates", [P, TILES, 3 * HEADS])
    q_st = sb("q_st", [P, KV_GROUPS, SEQ])
    prob = [sb(f"prob{i}", [P, S_COLS]) for i in range(2)]
    pT = [sb(f"probT{i}", [P, 4, P]) for i in range(4)]
    nmax = [sb(f"nmax{i}", [P, 3]) for i in range(2)]
    sums = [sb(f"sums{i}", [P, 3]) for i in range(2)]
    coef = [sb(f"coef{i}", [P, 3]) for i in range(2)]
    y_un = [sb(f"y_un{i}", [P, HD]) for i in range(2)]

    bank = lambda i: psum[:, i * 512:(i + 1) * 512]
    psT = [bank(4), bank(5)]
    psO = [bank(6), bank(7)]

    n_groups = [len(tile_groups(u // 2)) for u in range(UNITS)]
    before = [sum(n_groups[:u]) for u in range(UNITS + 1)]
    G = before[UNITS]
    assert G % 4 == 0

    s_ld = sem("consts_loaded")
    s_w1 = [sem(f"cmp_w_loaded{i}") for i in range(2)]
    s_kk = [sem(f"cmp_in_moved{i}") for i in range(2)]
    s_posps, s_pos, s_zero = sem("cmp_pos_ps"), sem("cmp_pos_sb"), sem("cmp_zeroed")
    s_bps, s_hps, s_hb, s_hid, s_cps, s_cmp = (sem(n) for n in ("hid_bias_ps", "hid_ps", "hid_bias", "hidden",
                                                               "cmp_ps", "cmp_sb"))
    s_e, s_gate = sem("gate_exp"), sem("gates_ready")
    s_qst, s_qk, s_max, s_exp = sem("q_staged"), sem("scores_ps"), sem("max_ready"), sem("probs_ready")
    s_tr, s_evV, s_evA, s_av = sem("probT_ps"), sem("probT_even_sb"), sem("probT_odd_sb"), sem("out_ps")
    s_coef, s_comb, s_chain = sem("coef_ready"), sem("out_used"), sem("dve_chain2")

    block = ctx.enter_context(nc.Block())

    @block.sync
    def _(sp):
        for i, (pe_, w1_, w2_) in enumerate(((pe_k, w1_k, w2_k), (pe_v, w1_v, w2_v))):
            sp.dma_start(pos[i][:], pe_.rearrange("(l a) d -> l (a d)", a=2)).then_inc(s_w1[i], 16)
            sp.dma_start(w1[i][:], w1_.rearrange("(l p) h -> p l h", p=P)).then_inc(s_w1[i], 16)
            sp.dma_start(w2[i][:], w2_.rearrange("(m p) d -> p m d", p=P)).then_inc(s_w1[i], 16)

    @block.gpsimd
    def _(pool):
        pool.dma_start(masks[:], k_masks[:, 0:2, :]).then_inc(s_ld, 16)
        pool.dma_start(cmask[:], k_cmask).then_inc(s_ld, 16)
        pool.dma_start(kside[:], k_kside).then_inc(s_ld, 16)
        pool.dma_start(qside[:], k_qside).then_inc(s_ld, 16)
        pool.dma_start(visible[:], k_masks[:, 2, 0:3]).then_inc(s_ld, 16)
        nc.gpsimd.memset(kcT[:], 0.0).then_inc(s_zero, 1)
        nc.gpsimd.memset(vc[:], 0.0).then_inc(s_zero, 1)
        for i in range(2):
            nc.gpsimd.memset(prob[i][:, CMP0 + NCP:S_COLS], 0.0).then_inc(s_zero, 1)
        nc.gpsimd.memset(q_st[:], 0.0).then_inc(s_zero, 1)

    @block.tensor
    def _(pe):
        pe.wait_ge(s_w1[0], 48)
        nc.tensor.transpose(psO[0][:, 0:L2], pos[0][:], ident[0:L2, 0:L2])
        pe.wait_ge(s_w1[1], 48)
        nc.tensor.transpose(psO[0][:, L2:2 * L2], pos[1][:], ident[0:L2, 0:L2]).then_inc(s_posps, 1)
        pe.wait_ge(s_pos, 1)
        for i in range(2):
            for m in range(M2):
                n = M2 * i + m
                for l in range(L2):
                    last = nc.tensor.matmul(psO[1][:, n:n + 1], w1[i][:, l, m * P:(m + 1) * P], posT[:, i, l:l + 1],
                                            start=(l == 0), stop=(l == L2 - 1))
        last.then_inc(s_bps, 1)
        for i in range(2):
            pe.wait_ge(s_kk[i], 16 * 2 * KV_GROUPS)
            for m in range(M2):
                n = M2 * i + m
                for l in range(L2):
                    last = nc.tensor.matmul(bank(n)[:, 0:KV_GROUPS * N_CMP], w1[i][:, l, m * P:(m + 1) * P],
                                            kk[i][:, :, 2 * l:2 * l + CMP_STRIDE * (N_CMP - 1) + 1:CMP_STRIDE],
                                            start=(l == 0), stop=(l == L2 - 1))
                last.then_inc(s_hps, 1)
        pe.wait_ge(s_hid, 2 * M2)
        for g in range(KV_GROUPS):
            for m in range(M2):
                nc.tensor.matmul(psT[0][g * HALF:(g + 1) * HALF, 0:N_CMP], w2[0][:, m, :],
                                 hid[:, 0, m, g * N_CMP:(g + 1) * N_CMP], start=(m == 0), stop=(m == M2 - 1))
        for g in range(KV_GROUPS):
            for m in range(M2):
                last = nc.tensor.matmul(psT[1][0:N_CMP, g * HD:(g + 1) * HD], hid[:, 1, m, g * N_CMP:(g + 1) * N_CMP],
                                        w2[1][:, m, :], start=(m == 0), stop=(m == M2 - 1))
        last.then_inc(s_cps, 1)
        pe.wait_ge(s_cmp, 1)
        pe.wait_ge(s_ld, 80)

        def scores(j, u):
            qt, g = u // 2, u % 2
            first = first_window_tile(qt)
            q = q_st[:, g, qt * P:(qt + 1) * P]
            alibi = qside[:, g, qt * P:(qt + 1) * P]
            pe.wait_ge(s_exp, (j * UNITS + u) * 3)
            for b, c0, n in branches(qt):
                for s0, m in strips(c0, n):
                    key0 = s0 - c0 + (first * P if b == B_WIN else 0)
                    dst = psum[:, s0:s0 + m]
                    if b == B_CMP:
                        add = [(s0, cmask[:, qt, :])]
                        side, keys = kside[:, SEQ:SEQ + NCP], kcT[:]
                    else:
                        side = kside[:, key0:key0 + m]
                        keys = kT_all[:, KS if b == B_SLC else KW, key0:key0 + m]
                        add = [(c0 + n - P, masks[:, 0, :])]
                        if b == B_WIN and qt >= WIN_TILES:
                            add.append((c0, masks[:, 1, :]))
                        add = [(at, mask) for at, mask in add if s0 <= at < s0 + m]
                    nc.tensor.matmul(dst, alibi, side, start=True, stop=False)
                    for at, mask in add:
                        nc.tensor.matmul(psum[:, at:at + mask.shape[1]], ident_b[:], mask, start=False, stop=False)
                    last = nc.tensor.matmul(dst, q, keys, start=False, stop=True)
                last.then_inc(s_qk, 1)

        def transpose_group(j, u, k):
            qt, g = u // 2, u % 2
            at = before[u] + k
            tiles = tile_groups(qt)[k]
            pe.wait_ge(s_evA if at % 2 else s_evV, j * (G // 2) + at // 2)
            done = max({B_SLC: 1, B_WIN: 2, B_CMP: 3}[t[0]] for t in tiles)
            pe.wait_ge(s_exp, (j * UNITS + u) * 3 + done)
            for n, (b, c0, m, kt) in enumerate(tiles):
                last = nc.tensor.transpose(psT[at % 2][:, n * P:(n + 1) * P], prob[g][:, c0:c0 + P], ident[:])
            last.then_inc(s_tr, 1)

        def weigh_values(j, u, k):
            qt, g = u // 2, u % 2
            at = before[u] + k
            pe.wait_ge(s_evA if at % 2 else s_evV, j * (G // 2) + at // 2 + 1)
            if k == 0:
                pe.wait_ge(s_comb, j * UNITS + max(u - 1, 0))
            for n, (b, c0, m, kt) in enumerate(tile_groups(qt)[k]):
                if b == B_CMP:
                    v, start, stop = vc[0:m, g * HD:(g + 1) * HD], True, True
                else:
                    v = misc[:, kt, (b - B_SLC) * P + g * HD:(b - B_SLC) * P + (g + 1) * HD]
                    start, stop = kt == (0 if b == B_SLC else first_window_tile(qt)), kt == qt
                last = nc.tensor.matmul(psO[g][:, b * HD:(b + 1) * HD], pT[at % 4][0:m, n, :], v, start=start,
                                        stop=stop)
            if k == n_groups[u] - 1:
                last.then_inc(s_av, 1)

        with pe.Fori(0, REP) as j:
            pe.wait_ge(s_qst, j + 1)
            for u in range(UNITS + 1):
                if u < UNITS:
                    scores(j, u)
                if u >= 1:
                    n = n_groups[u - 1]
                    for k in range(n + 1):
                        if k < n:
                            transpose_group(j, u - 1, k)
                        if k >= 1:
                            weigh_values(j, u - 1, k - 1)

    def steps(u, parity):
        ks = [] if u == 0 else [k for k in range(n_groups[u - 1]) if (before[u - 1] + k) % 2 == parity]
        order = []
        for n in range(max(3 if u < UNITS else 0, len(ks))):
            if n < 3 and u < UNITS:
                order.append(("part", n))
            if n < len(ks):
                order.append(("copy", ks[n]))
        return order

    def copy_group(eng, copy, s_ev, j, u, k):
        at = before[u] + k
        tiles = tile_groups(u // 2)[k]
        n = len(tiles)
        eng.wait_ge(s_tr, j * G + at + 1)
        copy(pT[at % 4][:, 0:n, :], psT[at % 2][:, 0:n * P].rearrange("p (n q) -> p n q", q=P)).then_inc(s_ev, 1)

    @block.scalar
    def _(act):
        for i, src in ((0, KC), (1, VC)):
            for g in range(KV_GROUPS):
                rows = kT_all[g * HALF:(g + 1) * HALF, src, :]
                act.dma_start(kk[i][0:HALF, g, :], rows).then_inc(s_kk[i], 16)
                act.dma_start(kk[i][HALF:P, g, 0:SEQ - 1], rows[:, 1:SEQ]).then_inc(s_kk[i], 16)
        for n in range(2 * M2):
            act.wait_ge(s_hb, 1)
            act.wait_ge(s_hps, n + 1)
            nc.scalar.activation(hid[:, n // M2, n % M2, :], bank(n)[:, 0:KV_GROUPS * N_CMP], ACT.Gelu_apprx_tanh,
                                 bias=hid_b[:, n:n + 1]).then_inc(s_hid, 1)
        nc.scalar.activation(gates[:], misc[:, :, 2 * P:MISC], ACT.Exp, scale=-1.0).then_inc(s_e, 1)

        with act.Fori(0, REP) as j:
            for u in range(UNITS + 1):
                for what, n in steps(u, 1):
                    if what == "part":
                        qt, g = u // 2, u % 2
                        b, c0, m = branches(qt)[n]
                        act.wait_ge(s_max, (j * UNITS + u) * 3 + (1 if n == 0 else 3))
                        if n == 0:
                            act.wait_ge(s_tr, j * G + before[max(u - 1, 0)])
                            act.wait_ge(s_coef, j * UNITS + max(u - 1, 0))
                        nc.scalar.activation(prob[g][:, c0:c0 + m], psum[:, c0:c0 + m], ACT.Exp,
                                             bias=nmax[g][:, b:b + 1],
                                             accum_out=sums[g][:, b:b + 1]).then_inc(s_exp, 1)
                    else:
                        copy_group(act, nc.scalar.copy, s_evA, j, u - 1, n)

    @block.vector
    def _(dve):
        ch = Chain(dve, s_chain)
        ch.link(nc.vector.tensor_copy(ident_b[:], ident[:]))
        dve.wait_ge(s_posps, 1)
        nc.vector.tensor_copy(posT[:], psO[0][:, 0:2 * L2].rearrange("p (i l) -> p i l", i=2)).then_inc(s_pos, 1)
        dve.wait_ge(s_bps, 1)
        nc.vector.tensor_copy(hid_b[:], psO[1][:, 0:2 * M2]).then_inc(s_hb, 1)
        dve.wait_ge(s_zero, 5)
        dve.wait_ge(s_cps, 1)
        nc.vector.tensor_copy(kcT[:, 0:N_CMP], psT[0][:, 0:N_CMP])
        nc.vector.tensor_copy(vc[0:N_CMP, :], psT[1][0:N_CMP, 0:P]).then_inc(s_cmp, 1)
        dve.wait_ge(s_e, 1)
        ch.link(nc.vector.tensor_scalar(gates[:], gates[:], 1.0, None, ALU.add))
        ch.link(nc.vector.reciprocal(gates[:], gates[:]))
        dve.wait_ge(s_ld, 80)
        SETUP = ch.n
        LINKS = UNITS * 4 + KV_GROUPS

        def row_max(j, u, n):
            qt, g = u // 2, u % 2
            b, c0, m = branches(qt)[n]
            dve.wait_ge(s_qk, (j * UNITS + u) * 3 + (1 if n == 0 else 3))
            nc.vector.tensor_reduce(nmax[g][:, b:b + 1], psum[:, c0:c0 + m], AX.X, ALU.max,
                                    negate=True).then_inc(s_max, 1)

        def weights_of_branches(j, u):
            qt, g = u // 2, u % 2
            dve.wait_ge(s_exp, (j * UNITS + u) * 3 + 3)
            dve.wait_ge(s_comb, j * UNITS + max(u - 1, 0))
            ch.link(nc.vector.tensor_scalar(coef[g][:], sums[g][:], 1e-30, None, ALU.max))
            ch.link(nc.vector.reciprocal(coef[g][:], coef[g][:]))
            if qt == 0:
                ch.link(nc.vector.tensor_tensor(coef[g][:], coef[g][:], visible[:], ALU.mult))
            nc.vector.tensor_tensor(coef[g][:], coef[g][:],
                                    gates[:, qt, bass.ds(g * 3 * REP + 3 * j, 3)], ALU.mult).then_inc(s_coef, 1)

        def add_branches(j, u):
            qt, g = u // 2, u % 2
            dve.wait_ge(s_coef, j * UNITS + u + 1)
            dve.wait_ge(s_av, j * UNITS + u + 1)
            o = [psO[g][:, b * HD:(b + 1) * HD] for b in range(3)]
            ch.link(nc.vector.tensor_scalar(y_un[g][:], o[0], coef[g][:, 0:1], None, ALU.mult))
            ch.link(nc.vector.scalar_tensor_tensor(y_un[g][:], o[1], coef[g][:, 1:2], y_un[g][:], ALU.mult, ALU.add))
            nc.vector.scalar_tensor_tensor(y_rows[:, qt, bass.ds(GM_WIDTH + g * REP * HD + j * HD, HD)], o[2],
                                           coef[g][:, 2:3], y_un[g][:], ALU.mult, ALU.add).then_inc(s_comb, 1)

        with dve.Fori(0, REP) as j:
            ch.at(SETUP + LINKS * j)
            dve.wait_ge(s_qk, j * UNITS * 3)
            for g in range(KV_GROUPS):
                half = slice(g * HALF, (g + 1) * HALF)
                last = nc.vector.tensor_scalar(q_st[half, g, :],
                                               qT_all[half, bass.ds(j, 1), :].rearrange("p a n -> p (a n)"), 1.0,
                                               None, ALU.mult)
            last.then_inc(s_qst, 1)
            for u in range(UNITS + 1):
                for what, n in steps(u, 0):
                    if what == "part":
                        row_max(j, u, n)
                    else:
                        copy_group(dve, nc.vector.tensor_copy, s_evV, j, u - 1, n)
                if u >= 1:
                    weights_of_branches(j, u - 1)
                    add_branches(j, u - 1)
            dve.wait_ge(s_qk, (j + 1) * UNITS * 3)
            nc.vector.tensor_scalar(qside[:], qside[:], 0.5, None, ALU.mult)
            assert ch.n == LINKS


def route(nc, ctx, sem, psum, x, w_out, w_router, b_router, k_upper, k_expert, k_pairs, mod_d, list_d, pass_d, x1_d,
          xn_d, ident, mod_t, scale2, y_rows, wts):
    sb = lambda name, shape, dt=f32: ctx.enter_context(nc.sbuf_tensor(name, shape, dt))
    two = lambda name, shape, dt=f32: [sb(f"{name}{i}", shape, dt) for i in range(2)]
    wo = sb("w_out_sb", [P, KD, D])
    wr = sb("w_router_sb", [P, KD, E])
    br = sb("b_router_sb", [P, E])
    gate1 = sb("gate1", [P, D])
    upper = sb("upper", [P, P], bf16)
    ones = sb("ones", [P, P], bf16)
    consts = sb("expert_consts", [P, 2 * E + 1])
    iota_e, list_base, iota_p = consts[:, 0:E], consts[:, E:2 * E], consts[:, 2 * E:2 * E + 1]
    sentinel = sb("sentinel", [P, LIST_ROWS // P, 2], i32)
    pairs_f = sb("pairs_f", [P, TOPK, 2])
    pairs_step = sb("pairs_step", [P, TOPK, 2])
    y_st = two("y_st", [P, D])
    mT = two("mixT", [P, KD, P])
    xr = two("x_rows_in", [P, D])
    x1 = two("x1", [P, D])
    xn = two("xn", [P, D])
    h2T = two("h2T", [P, KD, P])
    sq = sb("sq3", [P, D], bf16)
    ms = two("ms3_", [P, 1])
    rstd = two("rstd3_", [P, 1])
    consts2 = sb("eps_nhalf", [P, 2])
    tick = sb("tick3", [P, 1])
    lg = two("logits", [P, E])
    top = two("top", [P, 8])
    idx = two("top_idx", [P, 8], u32)
    idf = two("top_idf", [P, 8])
    neg0 = two("neg_top", [P, 1])
    below = two("below_top", [P, TOPK])
    wexp = two("wexp", [P, TOPK])
    wsum = two("wsum", [P, 1])
    winv = two("winv", [P, 1])
    hot = two("hot", [P, TOPK, E])
    mask = two("mask", [P, E])
    mask_b = two("mask_b", [P, E], bf16)
    total = sb("total", [P, E])
    total_b = two("total_b", [P, E], bf16)
    place = sb("place", [P, E])
    prod = sb("prod", [P, TOPK, E])
    slot_f = sb("slot_f", [P, TOPK])
    slot = two("slot", [P, TOPK], i32)
    pairs = two("pairs", [P, TOPK, 2], i32)
    tab = sb("tab", [P, 8, E])
    cols = sb("cols", [P, 8])
    table_f = sb("table_f", [P, PASS_COLS])
    table = sb("table", [P, PASS_COLS], i32)

    bank = lambda i: psum[:, i * 512:(i + 1) * 512]
    psY, psO, psX, psL, psC = (bank(0), bank(1)), (bank(2), bank(3)), (bank(4), bank(5)), bank(6), bank(7)

    s_w, s_c, s_cc = sem("w_out_loaded"), sem("consts3_loaded"), sem("consts3_cast")
    s_x = [sem(f"x3_loaded{i}") for i in range(2)]
    s_sent, s_mem, s_first = sem("list_cleared"), sem("sentinel_set"), sem("running_cleared")
    s_yst, s_yps, s_mT, s_mix, s_x1 = (sem(n) for n in ("y_staged", "yT_ps", "mixT_sb", "mix_ps", "x1_ready"))
    s_ms, s_mse, s_rstd, s_xn, s_xps, s_h2 = (sem(n) for n in ("ms3_ready", "ms3_eps", "rstd3_ready", "xn_ready",
                                                              "xnT_ps", "h2T_sb"))
    s_x1st = [sem(f"x1_stored{i}") for i in range(2)]
    s_xnst = [sem(f"xn_stored{i}") for i in range(2)]
    s_lg, s_neg, s_wexp, s_mask, s_posps, s_slot = (sem(n) for n in ("logits_ps", "neg_top_ready", "wexp_ready",
                                                                    "mask_ready", "place_ps", "slots_ready"))
    s_sc = [sem(f"list_scattered{i}") for i in range(2)]
    s_tick = sem("tick3_set")
    s_chain, s_cnt, s_tab, s_tabst = sem("dve_chain3"), sem("counts_ps"), sem("table_ready"), sem("table_stored")

    x_t = x.rearrange("(t p) d -> t p d", p=P)
    x1_t = x1_d.rearrange("(t p) d -> t p d", p=P)
    xn_t = xn_d.rearrange("(t p) d -> t p d", p=P)
    row = lambda ap_t, t: ap_t[bass.ds(t, 1)].rearrange("a p d -> (a p) d")

    def tiles(eng, body):
        body(0, 0, 0, 0, True)
        body(1, 1, 0, 1, True)
        with eng.Fori(1, TILES // 2 - 1) as i:
            body(2 * i, 0, i, 2, True)
            body(2 * i + 1, 1, i, 2, True)
        body(TILES - 2, 0, TILES // 2 - 1, 2, True)
        body(TILES - 1, 1, TILES // 2 - 1, 2, False)

    block = ctx.enter_context(nc.Block())

    @block.sync
    def _(sp):
        sp.dma_start(gate1[:], mod_d[2 * D:3 * D].rearrange("(a n) -> a n", a=1).partition_broadcast(P)).then_inc(s_c, 16)
        sp.dma_start(wr[:], w_router.rearrange("(k p) e -> p k e", p=P)).then_inc(s_c, 16)
        sp.dma_start(br[:], b_router.rearrange("(a n) -> a n", a=1).partition_broadcast(P)).then_inc(s_c, 16)
        sp.dma_start(consts[:], k_expert).then_inc(s_c, 16)
        sp.dma_start(pairs_f[:], k_pairs).then_inc(s_c, 16)
        sp.dma_start(wo[:], w_out.rearrange("(k p) n -> p k n", p=P)).then_inc(s_w, 16)
        for t in range(2):
            sp.dma_start(xr[t][:], x_t[t]).then_inc(s_x[t], 16)
        sp.wait_ge(s_mem, 1)
        sp.dma_start(list_d.rearrange("(p n) two -> p n two", p=P), sentinel[:]).then_inc(s_sent, 16)

        def body(t, par, i, back, nxt):
            sp.wait_ge(s_x1, t + 1)
            sp.dma_start(row(x1_t, t), x1[par][:]).then_inc(s_x1st[par], 16)
            if not (isinstance(t, int) and t >= TILES - 2):
                sp.dma_start(xr[par][:], row(x_t, t + 2)).then_inc(s_x[par], 16)
            sp.wait_ge(s_xn, t + 1)
            sp.dma_start(row(xn_t, t), xn[par][:]).then_inc(s_xnst[par], 16)
        tiles(sp, body)
        sp.wait_ge(s_tab, 1)
        sp.dma_start(pass_d, table[:]).then_inc(s_tabst, 16)
        sp.wait_ge(s_tabst, 16)
        for i in range(2):
            sp.wait_ge(s_x1st[i], 16 * TILES // 2)
            sp.wait_ge(s_xnst[i], 16 * TILES // 2)

    @block.gpsimd
    def _(pool):
        nc.gpsimd.memset(sentinel[:], TOPK * SEQ).then_inc(s_mem, 1)
        nc.gpsimd.memset(consts2[:, 0:1], EPS).then_inc(s_first, 1)
        nc.gpsimd.memset(consts2[:, 1:2], -0.5).then_inc(s_first, 1)
        nc.gpsimd.memset(total[:], 0.0).then_inc(s_first, 1)
        nc.gpsimd.memset(total_b[0][:], 0.0).then_inc(s_first, 1)
        nc.gpsimd.memset(ones[:], 1.0).then_inc(s_first, 1)
        nc.gpsimd.memset(pairs_step[:, :, 0:1], TOPK * P).then_inc(s_first, 1)
        nc.gpsimd.memset(pairs_step[:, :, 1:2], P).then_inc(s_first, 1)
        pool.dma_start(upper[:], k_upper).then_inc(s_cc, 16)
        pool.wait_ge(s_first, 7)

        def rms(t, par):
            pool.wait_ge(s_ms, t + 1)
            nc.gpsimd.tensor_tensor(ms[par][:], ms[par][:], consts2[:, 0:1], ALU.add).then_inc(s_mse, 1)
            pool.wait_ge(s_mse, t + 1)
            nc.gpsimd.tensor_tensor(rstd[par][:], ms[par][:], consts2[:, 1:2], ALU.pow).then_inc(s_rstd, 1)

        def scatter(t, par):
            pool.wait_ge(s_slot, t + 1)
            pool.wait_ge(s_sent, 16)
            pool.wait_ge(s_tick, t)
            nc.gpsimd.tensor_tensor(tick[:], consts2[:, 0:1], consts2[:, 1:2], ALU.add).then_inc(s_tick, 1)
            for k in range(TOPK):
                nc.gpsimd.indirect_dma_start(list_d, bass.IndirectOffsetOnAxis(ap=slot[par][:, k:k + 1], axis=0),
                                             pairs[par][:, k, :], None).then_inc(s_sc[par], 16)

        def body(t, par, i, back, nxt):
            rms(t, par)
            if back == 2:
                scatter(t - 2, par)
        tiles(pool, body)
        scatter(TILES - 2, 0)
        scatter(TILES - 1, 1)
        for i in range(2):
            pool.wait_ge(s_sc[i], 16 * TOPK * TILES // 2)

    @block.tensor
    def _(pe):
        def transpose_mix(t, par):
            pe.wait_ge(s_yst, t + 1)
            pe.wait_ge(s_mT, t)
            for k in range(KD):
                last = nc.tensor.transpose(psY[k // 4][:, (k % 4) * P:(k % 4 + 1) * P],
                                           y_st[par][:, k * P:(k + 1) * P], ident[:])
            last.then_inc(s_yps, 1)

        def project(t, par):
            pe.wait_ge(s_mT, t + 1)
            pe.wait_ge(s_x1, t)
            for n in range(2):
                for k in range(KD):
                    last = nc.tensor.matmul(psO[n], mT[par][:, k, :], wo[:, k, n * 512:(n + 1) * 512],
                                            start=(k == 0), stop=(k == KD - 1))
            last.then_inc(s_mix, 1)

        def logits(t, par):
            pe.wait_ge(s_xn, t + 1)
            pe.wait_ge(s_h2, t)
            for k in range(KD):
                last = nc.tensor.transpose(psX[k // 4][:, (k % 4) * P:(k % 4 + 1) * P],
                                           xn[par][:, k * P:(k + 1) * P], ident[:])
            last.then_inc(s_xps, 1)
            pe.wait_ge(s_h2, t + 1)
            pe.wait_ge(s_mask, t)
            for k in range(KD):
                last = nc.tensor.matmul(psL[:, 0:E], h2T[par][:, k, :], wr[:, k, :], start=(k == 0),
                                        stop=(k == KD - 1))
            last.then_inc(s_lg, 1)

        def places(t, par):
            pe.wait_ge(s_mask, t + 1)
            pe.wait_ge(s_slot, t)
            nc.tensor.matmul(psC[:, 0:E], upper[:], mask_b[par][:], start=True, stop=False)
            nc.tensor.matmul(psC[:, 0:E], ones[:], total_b[par][:], start=False, stop=True).then_inc(s_posps, 1)

        transpose_mix(0, 0)
        pe.wait_ge(s_w, 16)
        pe.wait_ge(s_cc, 16)

        def body(t, par, i, back, nxt):
            if nxt:
                transpose_mix(t + 1, 1 - par)
            project(t, par)
            if back == 2:
                places(t - 2, par)
            if back:
                logits(t - 1, 1 - par)
        tiles(pe, body)
        places(TILES - 2, 0)
        logits(TILES - 1, 1)
        places(TILES - 1, 1)
        pe.wait_ge(s_slot, TILES)
        nc.tensor.matmul(psC[:, 0:E], ones[:], total_b[0][:], start=True, stop=True).then_inc(s_cnt, 1)

    @block.scalar
    def _(act):
        def copy_mix(t, par):
            act.wait_ge(s_yps, t + 1)
            for n in range(2):
                last = nc.scalar.copy(mT[par][:, 4 * n:4 * n + 4, :], psY[n].rearrange("p (k q) -> p k q", q=P))
            last.then_inc(s_mT, 1)

        def mean_square(t, par):
            act.wait_ge(s_x1, t + 1)
            if not isinstance(t, int) or t >= 1:
                act.wait_ge(s_ms, t)
            if not isinstance(t, int) or t >= 2:
                act.wait_ge(s_rstd, t - 1)
            nc.scalar.activation(sq[:], x1[par][:], ACT.Square, scale=D ** -0.5, accum_out=ms[par][:]).then_inc(s_ms, 1)

        def weights(t, par):
            act.wait_ge(s_neg, t + 1)
            nc.scalar.activation(wexp[par][:], below[par][:], ACT.Exp, accum_out=wsum[par][:]).then_inc(s_wexp, 1)

        copy_mix(0, 0)

        def body(t, par, i, back, nxt):
            if nxt:
                copy_mix(t + 1, 1 - par)
            mean_square(t, par)
            if back:
                weights(t - 1, 1 - par)
        tiles(act, body)
        weights(TILES - 1, 1)

    @block.vector
    def _(dve):
        ch = Chain(dve, s_chain)

        def stage_mix(t, par):
            nc.vector.tensor_scalar(y_st[par][:], y_rows[:, bass.ds(t, 1), :].rearrange("p a n -> p (a n)"), 1.0, None,
                                    ALU.mult).then_inc(s_yst, 1)

        def residual(t, par):
            dve.wait_ge(s_mix, t + 1)
            for n in range(2):
                c = slice(n * 512, (n + 1) * 512)
                last = nc.vector.tensor_tensor(x1[par][:, c], psO[n], gate1[:, c], ALU.mult)
            ch.link(last)
            nc.vector.tensor_tensor(x1[par][:], x1[par][:], xr[par][:], ALU.add).then_inc(s_x1, 1)

        def normalise(t, par):
            dve.wait_ge(s_rstd, t + 1)
            nc.vector.tensor_scalar(xn[par][:], x1[par][:], rstd[par][:], None, ALU.mult).then_inc(s_xn, 1)

        def modulate_x(t, par):
            dve.wait_ge(s_xps, t + 1)
            for k in range(KD):
                last = nc.vector.tensor_scalar(h2T[par][:, k, :], psX[k // 4][:, (k % 4) * P:(k % 4 + 1) * P],
                                               scale2[:, k:k + 1], mod_t[:, 3 * KD + k:3 * KD + k + 1], ALU.mult,
                                               ALU.add)
            last.then_inc(s_h2, 1)

        def choose(t, par):
            dve.wait_ge(s_lg, t + 1)
            ch.link(nc.vector.tensor_tensor(lg[par][:], psL[:, 0:E], br[:], ALU.add))
            nc.vector.tensor_reduce(neg0[par][:], lg[par][:], AX.X, ALU.max, negate=True)
            ch.link(nc.vector.max(top[par][:], lg[par][:]))
            nc.vector.tensor_scalar(below[par][:], top[par][:, 0:TOPK], neg0[par][:], None, ALU.add).then_inc(s_neg, 1)
            ch.link(nc.vector.max_index(idx[par][:], top[par][:], lg[par][:]))
            ch.link(nc.vector.tensor_copy(idf[par][:], idx[par][:]))
            ch.link(nc.vector.tensor_tensor(hot[par][:], bc_mid(iota_e, TOPK), bc_last(idf[par][:, 0:TOPK], E),
                                            ALU.is_equal))
            ch.link(nc.vector.tensor_reduce(mask[par][:], hot[par][:].rearrange("p k e -> p e k"), AX.X, ALU.add))
            ch.link(nc.vector.tensor_tensor(total[:], total[:], mask[par][:], ALU.add))
            nc.vector.tensor_copy(total_b[1 - par][:], total[:])
            nc.vector.tensor_copy(mask_b[par][:], mask[par][:]).then_inc(s_mask, 1)
            dve.wait_ge(s_wexp, t + 1)
            ch.link(nc.vector.reciprocal(winv[par][:], wsum[par][:]))
            nc.vector.tensor_scalar(wts[:, bass.ds(t, 1), :].rearrange("p a k -> p (a k)"), wexp[par][:],
                                    winv[par][:], None, ALU.mult)

        def assign(t, par):
            dve.wait_ge(s_posps, t + 1)
            ch.link(nc.vector.tensor_tensor(place[:], psC[:, 0:E], list_base, ALU.add))
            ch.link(nc.vector.tensor_tensor(prod[:], hot[par][:], bc_mid(place[:], TOPK), ALU.mult))
            ch.link(nc.vector.tensor_reduce(slot_f[:], prod[:], AX.X, ALU.add))
            if not isinstance(t, int) or t >= 2:
                dve.wait_ge(s_sc[par], (16 * TOPK * (t // 2) if isinstance(t, int) else 16 * TOPK * t_half[0]))
            ch.link(nc.vector.tensor_copy(slot[par][:], slot_f[:]))
            dve.wait_ge(s_slot, t)
            ch.link(nc.vector.tensor_tensor(pairs_f[:], pairs_f[:], pairs_step[:], ALU.add))
            nc.vector.tensor_copy(pairs[par][:], pairs_f[:]).then_inc(s_slot, 1)

        t_half = [0]
        stage_mix(0, 0)
        stage_mix(1, 1)
        dve.wait_ge(s_c, 80)
        dve.wait_ge(s_first, 7)
        N1 = 1
        NR, NS = 8, 5

        def base(t):
            return (N1 + NR + NS) * t - NR - 2 * NS if not isinstance(t, int) else (
                N1 * t + NR * max(t - 1, 0) + NS * max(t - 2, 0))

        def body(t, par, i, back, nxt):
            ch.at(base(t))
            dve.wait_ge(s_x[par], 16 * (i + 1))
            if not isinstance(t, int) or t >= 2:
                dve.wait_ge(s_x1st[par], 16 * i)
                dve.wait_ge(s_xnst[par], 16 * i)
            residual(t, par)
            if back == 2:
                t_half[0] = i - 1
                assign(t - 2, par)
            normalise(t, par)
            if not (isinstance(t, int) and t >= TILES - 2):
                dve.wait_ge(s_yps, t + 1)
                stage_mix(t + 2, par)
            if back:
                modulate_x(t - 1, 1 - par)
                choose(t - 1, 1 - par)
        tiles(dve, body)
        assign(TILES - 2, 0)
        modulate_x(TILES - 1, 1)
        choose(TILES - 1, 1)
        assign(TILES - 1, 1)

        dve.wait_ge(s_cnt, 1)
        cnt, many, cum, le, tmp, hot_e, more = (tab[:, n, :] for n in range(7))
        col = lambda n: cols[:, n:n + 1]
        ch.link(nc.vector.tensor_copy(cnt, psC[:, 0:E]))
        ch.link(nc.vector.tensor_scalar(many, cnt, float(CAP), 1.0, ALU.is_gt, ALU.add))
        for n in range(2, -(-SEQ // CAP)):
            ch.link(nc.vector.tensor_scalar(more, cnt, float(n * CAP), None, ALU.is_gt))
            ch.link(nc.vector.tensor_tensor(many, many, more, ALU.add))
        ch.link(nc.vector.tensor_scalar(tmp, cnt, 0.0, None, ALU.mult))
        ch.link(nc.vector.tensor_tensor_scan(cum, many, tmp, 0.0, ALU.add, ALU.add))
        ch.link(nc.vector.tensor_scalar(le, cum, iota_p, None, ALU.is_le))
        ch.link(nc.vector.tensor_reduce(col(0), le, AX.X, ALU.add))
        ch.link(nc.vector.tensor_tensor(tmp, le, many, ALU.mult))
        ch.link(nc.vector.tensor_reduce(col(1), tmp, AX.X, ALU.add))
        ch.link(nc.vector.tensor_scalar(col(2), iota_p, col(1), float(CAP), ALU.subtract, ALU.mult))
        ch.link(nc.vector.tensor_scalar(hot_e, iota_e, col(0), None, ALU.is_equal))
        ch.link(nc.vector.tensor_tensor(more, hot_e, cnt, ALU.mult))
        ch.link(nc.vector.tensor_reduce(col(3), more, AX.X, ALU.add))
        tf = lambda n: table_f[:, n:n + 1]
        ch.link(nc.vector.tensor_scalar(col(4), col(3), col(2), None, ALU.subtract))
        ch.link(nc.vector.memset(table_f[:], 0.0))
        ch.link(nc.vector.tensor_scalar(tf(T_EXPERT), col(0), float(E - 1), None, ALU.min))
        ch.link(nc.vector.tensor_scalar(tf(T_START), col(0), float(SLOTS), col(2), ALU.mult, ALU.add))
        ch.link(nc.vector.tensor_scalar(tf(T_START), tf(T_START), float(E * SLOTS), None, ALU.min))
        for out_col, step in ((T_WIDTH, STEP), (T_SUBS, P)):
            ch.link(nc.vector.tensor_scalar(tf(out_col), col(4), float(P), 1.0, ALU.is_gt, ALU.add))
            for at in range(P + step, CAP, step):
                ch.link(nc.vector.tensor_scalar(col(5), col(4), float(at), None, ALU.is_gt))
                ch.link(nc.vector.tensor_tensor(tf(out_col), tf(out_col), col(5), ALU.add))
        ch.link(nc.vector.tensor_copy(tf(T_PASSES), tab[:, 2, E - 1:E]))
        nc.vector.tensor_copy(table[:], table_f[:]).then_inc(s_tab, 1)


def experts(nc, ctx, sem, psum, w_gate_up, b_gate_up, w_down, b_down, list_d, pass_d, xn_d, y_d, ident, mod_t, scale2):
    sb = lambda name, shape, dt=f32: ctx.enter_context(nc.sbuf_tensor(name, shape, dt))
    two = lambda name, shape, dt=f32: [sb(f"{name}{i}", shape, dt) for i in range(2)]
    COLS = 4 * P
    UP_SLOTS, DOWN_SLOTS = 2 * D // COLS, D // COLS
    wg = [sb(f"w_gu{s}", [P, KD, COLS]) for s in range(UP_SLOTS)]
    wd = [sb(f"w_dn{s}", [P, KD, COLS]) for s in range(DOWN_SLOTS)]
    xg = sb("x_gathered", [P, SUBS, D])
    xT = sb("xT", [P, KD, CAP])
    actT = sb("actT", [P, KD, CAP])
    yT = two("yT", [P, CAP])
    y_out = sb("y_out", [P, SUBS, D])
    glu = two("glu", [P, CAP])
    lin = two("lin", [P, CAP])
    sig = two("sig", [P, CAP])
    b_rows = sb("b_rows", [E, 3 * D])
    biasT = sb("biasT", [P, 3 * KD, E])
    bias = sb("bias", [P, 3 * KD])
    ptab = sb("ptab", [1, P * PASS_COLS], i32)
    zero = sb("zero", [P, 1])
    tick = two("tick4_", [P, 1])
    ids_g = sb("ids_gather", [P, SUBS, 2], i32)
    ids_s = sb("ids_scatter", [P, SUBS, 2], i32)

    bank = lambda i: psum[:, i * 512:(i + 1) * 512]
    psG, psL, psX, psY = (bank(0), bank(2)), (bank(1), bank(3)), (bank(4), bank(5)), (bank(6), bank(7))

    s_tab, s_b, s_bps, s_bT, s_clear = (sem(n) for n in ("ptab_loaded", "b_loaded", "b_ps", "biasT_ready",
                                                        "buffers_cleared"))
    s_w = [sem(f"w_loaded{s}") for s in range(UP_SLOTS + DOWN_SLOTS)]
    s_idg, s_ids, s_xg, s_ysc = sem("ids_g_loaded"), sem("ids_s_loaded"), sem("x_gathered"), sem("y_scattered")
    s_tick = [sem(f"tick4_set{i}") for i in range(2)]
    s_bias, s_xps, s_xT = sem("bias_ready"), sem("xT_ps4"), sem("xT_sb4")
    s_gu, s_gate, s_glu, s_sig, s_act = (sem(n) for n in ("gu_ps", "gu_used", "glu_ready", "sig_ready", "act_ready"))
    s_yps, s_yT, s_ytr, s_y = sem("y_ps"), sem("yT_sb"), sem("y_rows_ps"), sem("y_rows_sb")
    s_chain = sem("dve_chain4")

    wg_v = w_gate_up.rearrange("e (k p) n -> e p k n", p=P)
    wd_v = w_down.rearrange("e (k p) n -> e p k n", p=P)

    def passes(eng):
        eng.wait_ge(s_tab, 16)
        entry = lambda p, c, lo, hi: eng.value_load(ptab[0:1, bass.ds(PASS_COLS * p + c, 1)], min_val=lo, max_val=hi)
        count = eng.value_load(ptab[0:1, T_PASSES:T_PASSES + 1], min_val=E, max_val=MAX_PASSES)
        return count, entry

    def by_width(eng, width, body):
        for n, w in enumerate(WIDTHS):
            with eng.If(width == n + 1):
                body(w, -(-w // P))

    def by_subs(eng, subs, body):
        for n in range(1, SUBS + 1):
            with eng.If(subs == n):
                body(n)

    block = ctx.enter_context(nc.Block())

    @block.sync
    def _(sp):
        sp.dma_start(ptab[:], pass_d.rearrange("p c -> (p c)").rearrange("(a n) -> a n", a=1)).then_inc(s_tab, 16)
        sp.dma_start(b_rows[:, 0:2 * D], b_gate_up).then_inc(s_b, 16)
        sp.dma_start(b_rows[:, 2 * D:3 * D], b_down).then_inc(s_b, 16)
        count, entry = passes(sp)

        def load(e, s):
            dst, src, c = (wg[s], wg_v, s) if s < UP_SLOTS else (wd[s - UP_SLOTS], wd_v, s - UP_SLOTS)
            sp.dma_start(dst[:], src[bass.ds(e, 1), :, :, c * COLS:(c + 1) * COLS].rearrange("e p k n -> (e p) k n")
                         ).then_inc(s_w[s], 16)
        first = entry(0, T_EXPERT, 0, E - 1)
        for s in range(UP_SLOTS + DOWN_SLOTS):
            load(first, s)
        with sp.Fori(1, count) as p:
            e = entry(p, T_EXPERT, 0, E - 1)
            for s in range(UP_SLOTS + DOWN_SLOTS):
                if s < UP_SLOTS:
                    sp.wait_ge(s_gu, KD * (p - 1) + 2 * (s + 1))
                else:
                    sp.wait_ge(s_yps, KD * (p - 1) + 4 * (s - UP_SLOTS + 1))
                load(e, s)

    @block.gpsimd
    def _(pool):
        nc.gpsimd.memset(xg[:], 0.0).then_inc(s_clear, 1)
        nc.gpsimd.memset(y_out[:], 0.0).then_inc(s_clear, 1)
        nc.gpsimd.memset(yT[0][:], 0.0).then_inc(s_clear, 1)
        nc.gpsimd.memset(yT[1][:], 0.0).then_inc(s_clear, 1)
        nc.gpsimd.memset(zero[:], 0.0).then_inc(s_clear, 1)
        count, entry = passes(pool)
        pool.wait_ge(s_clear, 5)

        def fetch_ids(ids, start, s):
            pool.dma_start(ids[:], list_d[bass.ds(start, CAP), :].rearrange("(s p) two -> p s two", p=P)).then_inc(s, 16)

        def carry_waits(tick, s_tick, p):
            pool.wait_ge(s_tick, p)
            nc.gpsimd.tensor_tensor(tick[:], zero[:], zero[:], ALU.add).then_inc(s_tick, 1)

        def gather(p, start):
            fetch_ids(ids_g, start, s_idg)
            pool.wait_ge(s_idg, 16 * (p + 1))
            pool.wait_ge(s_xps, KD * p)
            carry_waits(tick[0], s_tick[0], p)
            for s in range(SUBS):
                nc.gpsimd.indirect_dma_start(xg[:, s, :], None, xn_d,
                                             bass.IndirectOffsetOnAxis(ap=ids_g[:, s, 1:2], axis=0),
                                             bounds_check=SEQ - 1, oob_is_err=False).then_inc(s_xg, 16)

        gather(0, entry(0, T_START, 0, E * SLOTS))
        with pool.Fori(0, count) as p:
            here, after = entry(p, T_START, 0, E * SLOTS), entry(p + 1, T_START, 0, E * SLOTS)
            pool.wait_ge(s_xg, 16 * SUBS * (p + 1))
            gather(p + 1, after)
            pool.wait_ge(s_ysc, 16 * SUBS * p)
            fetch_ids(ids_s, here, s_ids)
            pool.wait_ge(s_ids, 16 * (p + 1))
            pool.wait_ge(s_y, KD * (p + 1))
            carry_waits(tick[1], s_tick[1], p)
            for s in range(SUBS):
                nc.gpsimd.indirect_dma_start(y_d, bass.IndirectOffsetOnAxis(ap=ids_s[:, s, 0:1], axis=0),
                                             y_out[:, s, :], None, bounds_check=TOPK * SEQ - 1,
                                             oob_is_err=False).then_inc(s_ysc, 16)
        pool.wait_ge(s_ysc, count * (16 * SUBS))
        pool.wait_ge(s_xg, count * (16 * SUBS) + 16 * SUBS)

    @block.tensor
    def _(pe):
        pe.wait_ge(s_b, 32)
        for n in range(3 * KD):
            src = b_rows[:, (n // 2) * 2 * P + n % 2:(n // 2 + 1) * 2 * P:2] if n < 2 * KD else (
                b_rows[:, 2 * D + (n - 2 * KD) * P:2 * D + (n - 2 * KD + 1) * P])
            last = nc.tensor.transpose(bank(n // 16)[:, (n % 16) * E:(n % 16 + 1) * E], src, ident[0:E, 0:E])
        last.then_inc(s_bps, 1)
        count, entry = passes(pe)
        pe.wait_ge(s_bT, 1)

        def transpose_x(p, subs):
            def body(subs):
                pe.wait_ge(s_xg, 16 * SUBS * (p + 1))
                for c in range(KD):
                    pe.wait_ge(s_xT, KD * p + max(c - 1, 0))
                    for s in range(subs):
                        last = nc.tensor.transpose(psX[c % 2][:, s * P:(s + 1) * P], xg[:, s, c * P:(c + 1) * P],
                                                   ident[:])
                    last.then_inc(s_xps, 1)
            by_subs(pe, subs, body)

        transpose_x(0, entry(0, T_SUBS, 1, SUBS))
        with pe.Fori(0, count) as p:
            width, next_subs = entry(p, T_WIDTH, 1, len(WIDTHS)), entry(p + 1, T_SUBS, 1, SUBS)

            def up(w, subs):
                pe.wait_ge(s_xT, KD * (p + 1))
                pe.wait_ge(s_yT, KD * p)
                for f in range(KD):
                    if f % 2 == 0:
                        pe.wait_ge(s_w[f // 2], 16 * (p + 1))
                    if f >= 2:
                        pe.wait_ge(s_gate, KD * p + f - 1)
                    for ps, odd in ((psG[f % 2], 0), (psL[f % 2], 1)):
                        for k in range(KD):
                            last = nc.tensor.matmul(ps[:, 0:w], wg[f // 2][:, k, (f % 2) * 2 * P + odd:(f % 2 + 1) * 2 * P:2], xT[:, k, 0:w],
                                                    start=(k == 0), stop=(k == KD - 1))
                    last.then_inc(s_gu, 1)
            by_width(pe, width, up)
            transpose_x(p + 1, next_subs)

            def down(w, subs):
                pe.wait_ge(s_act, KD * (p + 1))

                def to_rows(m):
                    pe.wait_ge(s_yT, KD * p + m + 1)
                    pe.wait_ge(s_y, KD * p + max(m - 1, 0))
                    for s in range(subs):
                        last = nc.tensor.transpose(psY[m % 2][:, s * P:(s + 1) * P], yT[m % 2][:, s * P:(s + 1) * P],
                                                   ident[:])
                    last.then_inc(s_ytr, 1)
                for m in range(KD):
                    if m % 4 == 0:
                        pe.wait_ge(s_w[UP_SLOTS + m // 4], 16 * (p + 1))
                    if m >= 2:
                        pe.wait_ge(s_yT, KD * p + m - 1)
                    for k in range(KD):
                        last = nc.tensor.matmul(psG[m % 2][:, 0:w], wd[m // 4][:, k, (m % 4) * P:(m % 4 + 1) * P],
                                                actT[:, k, 0:w], start=(k == 0), stop=(k == KD - 1))
                    last.then_inc(s_yps, 1)
                    if m >= 1:
                        to_rows(m - 1)
                to_rows(KD - 1)
            by_width(pe, width, down)

    @block.scalar
    def _(act):
        count, entry = passes(act)

        def copy_x(p, subs):
            def body(subs):
                for c in range(KD):
                    act.wait_ge(s_xps, KD * p + c + 1)
                    nc.scalar.activation(xT[:, c, 0:subs * P], psX[c % 2][:, 0:subs * P], ACT.Identity,
                                         scale=scale2[:, c:c + 1],
                                         bias=mod_t[:, 3 * KD + c:3 * KD + c + 1]).then_inc(s_xT, 1)
            by_subs(act, subs, body)

        copy_x(0, entry(0, T_SUBS, 1, SUBS))
        with act.Fori(0, count) as p:
            width, next_subs = entry(p, T_WIDTH, 1, len(WIDTHS)), entry(p + 1, T_SUBS, 1, SUBS)

            def sigmoids(w, subs):
                for f in range(KD):
                    act.wait_ge(s_glu, KD * p + f + 1)
                    act.wait_ge(s_act, KD * p + max(f - 1, 0))
                    nc.scalar.activation(sig[f % 2][:, 0:w], glu[f % 2][:, 0:w], ACT.Sigmoid,
                                         scale=ALPHA).then_inc(s_sig, 1)
            by_width(act, width, sigmoids)
            copy_x(p + 1, next_subs)

            def outputs(w, subs):
                for m in range(KD):
                    act.wait_ge(s_yps, KD * p + m + 1)
                    act.wait_ge(s_ytr, KD * p + max(m - 1, 0))
                    nc.scalar.activation(yT[m % 2][:, 0:w], psG[m % 2][:, 0:w], ACT.Identity,
                                         bias=bias[:, 2 * KD + m:2 * KD + m + 1]).then_inc(s_yT, 1)
            by_width(act, width, outputs)

    @block.vector
    def _(dve):
        ch = Chain(dve, s_chain)
        dve.wait_ge(s_bps, 1)
        nc.vector.tensor_copy(biasT[:, 0:16, :], bank(0).rearrange("p (n e) -> p n e", e=E))
        nc.vector.tensor_copy(biasT[:, 16:24, :], bank(1)[:, 0:8 * E].rearrange("p (n e) -> p n e", e=E)
                              ).then_inc(s_bT, 1)
        dve.wait_ge(s_bT, 1)
        dve.wait_ge(s_clear, 5)
        count, entry = passes(dve)
        LINKS = 2 * KD
        with dve.Fori(0, count) as p:
            e = entry(p, T_EXPERT, 0, E - 1)
            width, subs = entry(p, T_WIDTH, 1, len(WIDTHS)), entry(p, T_SUBS, 1, SUBS)
            dve.wait_ge(s_yT, KD * p)
            nc.vector.tensor_scalar(bias[:], biasT[:, :, bass.ds(e, 1)].rearrange("p n a -> p (n a)"), 1.0, None,
                                    ALU.mult).then_inc(s_bias, 1)

            def gates(w, subs):
                dve.wait_ge(s_bias, p + 1)
                ch.at(LINKS * p)

                def clamp(f):
                    g, l = glu[f % 2][:, 0:w], lin[f % 2][:, 0:w]
                    dve.wait_ge(s_gu, KD * p + f + 1)
                    dve.wait_ge(s_act, KD * p + max(f - 1, 0))
                    nc.vector.tensor_scalar(g, psG[f % 2][:, 0:w], bias[:, 2 * f:2 * f + 1], LIMIT, ALU.add,
                                            ALU.min).then_inc(s_glu, 1)
                    nc.vector.tensor_scalar(l, psL[f % 2][:, 0:w], bias[:, 2 * f + 1:2 * f + 2], LIMIT, ALU.add,
                                            ALU.min).then_inc(s_gate, 1)
                    dve.wait_ge(s_gate, KD * p + f + 1)
                    ch.link(nc.vector.tensor_scalar(l, l, -LIMIT, 1.0, ALU.max, ALU.add))
                    ch.link(nc.vector.tensor_tensor(l, l, g, ALU.mult))

                def gate(f):
                    dve.wait_ge(s_sig, KD * p + f + 1)
                    nc.vector.tensor_tensor(actT[:, f, 0:w], lin[f % 2][:, 0:w], sig[f % 2][:, 0:w],
                                            ALU.mult).then_inc(s_act, 1)
                for f in range(KD):
                    clamp(f)
                    gate(f)
                assert ch.n == LINKS
            by_width(dve, width, gates)

            def rows(subs):
                dve.wait_ge(s_ysc, 16 * SUBS * p)
                for m in range(KD):
                    dve.wait_ge(s_ytr, KD * p + m + 1)
                    nc.vector.tensor_copy(y_out[:, 0:subs, m * P:(m + 1) * P],
                                          psY[m % 2][:, 0:subs * P].rearrange("p (s d) -> p s d", d=P)
                                          ).then_inc(s_y, 1)
            by_subs(dve, subs, rows)


def combine(nc, ctx, sem, g_final, mod_d, x1_d, y_d, wts, out):
    sb = lambda name, shape, dt=f32: ctx.enter_context(nc.sbuf_tensor(name, shape, dt))
    two = lambda name, shape, dt=f32: [sb(f"{name}{i}", shape, dt) for i in range(2)]
    gate2 = sb("gate2", [P, D])
    gf = sb("g_final_sb", [P, D])
    y4 = two("y4_", [P, TOPK, D])
    x1 = two("x1_5_", [P, D])
    acc = two("acc", [P, D])
    res = two("res", [P, D])
    sq = sb("sq5", [P, D], bf16)
    ms = two("ms5_", [P, 1])
    rstd = two("rstd5_", [P, 1])
    wcur = two("w_cur", [P, TOPK])
    consts = sb("eps_nhalf5", [P, 2])

    s_c, s_set = sem("consts5_loaded"), sem("eps5_set")
    s_y = [sem(f"y4_loaded{i}") for i in range(2)]
    s_x = [sem(f"x1_5_loaded{i}") for i in range(2)]
    s_out = [sem(f"out_stored{i}") for i in range(2)]
    s_first, s_acc, s_res, s_ms, s_mse, s_rstd, s_fin = (sem(n) for n in ("first_weighed", "summed", "res_ready",
                                                                         "ms5_ready", "ms5_eps", "rstd5", "final"))
    s_chain = sem("dve_chain5")
    y_t = y_d.rearrange("(t p k) d -> t p k d", p=P, k=TOPK)
    x1_t = x1_d.rearrange("(t p) d -> t p d", p=P)
    out_t = out.rearrange("(t p) d -> t p d", p=P)

    def tiles(eng, body):
        with eng.Fori(0, TILES // 2 - 1) as i:
            body(2 * i, 0, i, True)
            body(2 * i + 1, 1, i, True)
        body(TILES - 2, 0, TILES // 2 - 1, False)
        body(TILES - 1, 1, TILES // 2 - 1, False)

    block = ctx.enter_context(nc.Block())

    @block.sync
    def _(sp):
        def load(t, par):
            sp.dma_start(y4[par][:], y_t[bass.ds(t, 1)].rearrange("a p k d -> (a p) k d")).then_inc(s_y[par], 16)
            sp.dma_start(x1[par][:], x1_t[bass.ds(t, 1)].rearrange("a p d -> (a p) d")).then_inc(s_x[par], 16)
        load(0, 0)
        sp.dma_start(gate2[:], mod_d[5 * D:6 * D].rearrange("(a n) -> a n", a=1).partition_broadcast(P)
                     ).then_inc(s_c, 16)
        sp.dma_start(gf[:], g_final.rearrange("(a n) -> a n", a=1).partition_broadcast(P)).then_inc(s_c, 16)
        load(1, 1)

        def body(t, par, i, nxt2):
            if nxt2:
                sp.wait_ge(s_res, t + 1)
                load(t + 2, par)
            sp.wait_ge(s_fin, t + 1)
            sp.dma_start(out_t[bass.ds(t, 1)].rearrange("a p d -> (a p) d"), res[par][:]).then_inc(s_out[par], 16)
        tiles(sp, body)
        for i in range(2):
            sp.wait_ge(s_out[i], 16 * TILES // 2)

    @block.gpsimd
    def _(pool):
        nc.gpsimd.memset(consts[:, 0:1], EPS).then_inc(s_set, 1)
        nc.gpsimd.memset(consts[:, 1:2], -0.5).then_inc(s_set, 1)
        pool.wait_ge(s_set, 2)

        def body(t, par, i, nxt2):
            pool.wait_ge(s_ms, t + 1)
            nc.gpsimd.tensor_tensor(ms[par][:], ms[par][:], consts[:, 0:1], ALU.add).then_inc(s_mse, 1)
            pool.wait_ge(s_mse, t + 1)
            nc.gpsimd.tensor_tensor(rstd[par][:], ms[par][:], consts[:, 1:2], ALU.pow).then_inc(s_rstd, 1)
        tiles(pool, body)

    @block.scalar
    def _(act):
        def body(t, par, i, nxt2):
            act.wait_ge(s_res, t + 1)
            act.wait_ge(s_ms, t)
            act.wait_ge(s_rstd, t)
            nc.scalar.activation(sq[:], res[par][:], ACT.Square, scale=D ** -0.5, accum_out=ms[par][:]).then_inc(s_ms, 1)
        tiles(act, body)

    @block.vector
    def _(dve):
        ch = Chain(dve, s_chain)
        dve.wait_ge(s_c, 32)
        LINKS = TOPK + 2

        def finish(t, par):
            dve.wait_ge(s_rstd, t + 1)
            nc.vector.scalar_tensor_tensor(res[par][:], res[par][:], rstd[par][:], gf[:], ALU.mult,
                                           ALU.mult).then_inc(s_fin, 1)

        def body(t, par, i, nxt2):
            ch.at(LINKS * t)
            w = lambda k: wcur[par][:, k:k + 1]
            dve.wait_ge(s_y[par], 16 * (i + 1))
            dve.wait_ge(s_res, t)
            ch.link(nc.vector.tensor_scalar(wcur[par][:], wts[:, bass.ds(t, 1), :].rearrange("p a k -> p (a k)"), 1.0,
                                            None, ALU.mult))
            ch.link(nc.vector.tensor_scalar(acc[par][:], y4[par][:, 0, :], w(0), None, ALU.mult))
            for k in range(1, TOPK):
                ch.link(nc.vector.scalar_tensor_tensor(acc[par][:], y4[par][:, k, :], w(k), acc[par][:], ALU.mult,
                                                       ALU.add))
            ch.link(nc.vector.tensor_tensor(acc[par][:], acc[par][:], gate2[:], ALU.mult))
            dve.wait_ge(s_x[par], 16 * (i + 1))
            dve.wait_ge(s_out[par], 16 * i)
            nc.vector.tensor_tensor(res[par][:], acc[par][:], x1[par][:], ALU.add).then_inc(s_res, 1)
            finish(t, par)
        tiles(dve, body)


def kernel(**inputs):
    import concourse.bacc as bacc
    from concourse.bass_utils import run_bass_kernel_spmd

    nc = bacc.Bacc("TRN2", target_bir_lowering=False, num_devices=1)
    arrays, args = {}, []

    def add(name, a):
        a = np.ascontiguousarray(a)
        arrays[name] = a
        args.append(nc.dram_tensor(name, a.shape, mybir.dt.from_np(a.dtype), kind="ExternalInput").ap())
    for name in NAMES:
        a = np.asarray(inputs[name])
        add("in_" + name, a if name == "g_final" else a[0])
    for name, a in shape_constants().items():
        add(name, a)
    args.append(nc.dram_tensor("out_rows", [SEQ, D], f32, kind="ExternalOutput").ap())
    layer_kernel(nc, *args)
    r = run_bass_kernel_spmd(nc, [arrays], core_ids=[0])
    return r.results[0]["out_rows"].reshape(1, SEQ, D)


NAMES = ["x", "c", "w_ada", "b_ada", "g_mix_norm", "w_in", "gm_w_s", "gm_b_s", "gm_norm_g", "cmp_pe_k", "cmp_w1_k",
         "cmp_w2_k", "cmp_pe_v", "cmp_w1_v", "cmp_w2_v", "w_out", "g_ffn_norm", "w_router", "b_router", "w_gate_up",
         "b_gate_up", "w_down", "b_down", "g_final"]


def shape_constants():
    r = np.arange(P)
    t = np.arange(SEQ)
    masks = np.zeros((P, 3, P), np.float32)
    masks[:, 0] = np.where(r[None, :] <= r[:, None], 0.0, NEG)
    masks[:, 1] = np.where(r[None, :] > r[:, None], 0.0, NEG)
    masks[:, 2] = np.where((np.arange(P)[None, :] == B_CMP) & (r[:, None] < CMP_BLOCK - 1), 0.0, 1.0)
    block = np.arange(NCP)
    cend = block * CMP_STRIDE + CMP_BLOCK - 1
    seen = (cend[None, :] <= t[:, None]) & (block < N_CMP)[None, :]
    cmask = np.where(seen, 0.0, NEG).astype(np.float32).reshape(TILES, P, NCP).transpose(1, 0, 2)
    key = np.concatenate([t, block * CMP_STRIDE])
    low = np.concatenate([t % P, block * CMP_STRIDE % P + CMP_BLOCK - 1])
    kside = np.stack([low, key - key % P, np.ones_like(key), np.ones_like(key)]).astype(np.float32)
    qside = np.zeros((4, KV_GROUPS, SEQ), np.float32)
    for g in range(KV_GROUPS):
        slope = 2.0 ** (-8.0 * (g * REP + 1) / HEADS)
        qside[:, g] = slope * np.stack([np.ones(SEQ), np.ones(SEQ), -(t % P), -(t - t % P)])
    expert = np.zeros((P, 2 * E + 1), np.float32)
    expert[:, 0:E] = np.arange(E)
    expert[:, E:2 * E] = np.arange(E) * SLOTS
    expert[:, 2 * E] = r
    upper = (r[:, None] < r[None, :]).astype(np.float32)
    pairs = np.stack([4 * r[:, None] + np.arange(TOPK)[None, :], np.broadcast_to(r[:, None], (P, TOPK))], 2) - np.array([TOPK * P, P])
    return dict(k_ident=np.eye(P, dtype=np.float32), k_masks=masks, k_cmask=np.ascontiguousarray(cmask), k_kside=kside,
                k_qside=qside, k_upper=upper, k_expert=expert, k_pairs=pairs.astype(np.float32))
```
